# Optimizing a Trainium2 kernel written in Bass

```python
import math
import jax, jax.numpy as jnp
from jax import lax
import numpy as np

D_MODEL = 1024
BATCH = 1
SEQ = 256
DEPTH = 2

MEM_LEN = 256
A_HEADS = 4
A_HEAD_DIM = 64
A_WIDTH = A_HEADS * A_HEAD_DIM
CHUNK = 128
MLA_HEADS = 8
MLA_NOPE = 64
MLA_ROPE = 32
MLA_V = 64
Q_LORA = 256
KV_LORA = 128
MLA_WIDTH = MLA_HEADS * MLA_V
Q_BLOCK = 128
ROPE_BASE = 10000.0
C_WIDTH = 256
CONV_W = 3
D_WIDTH = 256
POOL_WINDOWS = (2, 4, 8, 16)
D_GROUP = D_WIDTH // len(POOL_WINDOWS)
MIX_WIDTH = A_WIDTH + MLA_WIDTH + C_WIDTH + D_WIDTH
P_A = 2 * A_WIDTH
P_B = Q_LORA + KV_LORA + MLA_ROPE
P_C = 3 * C_WIDTH
P_D = D_WIDTH
P_IN = P_A + P_B + P_C + P_D
X_HEADS = 4
X_HEAD_DIM = D_MODEL // X_HEADS
N_EXPERTS = 16
N_GROUPS = 4
EXPERTS_PER_GROUP = N_EXPERTS // N_GROUPS
TOP_K = 2
D_FF_EXPERT = 256
ALPHA = (2 * DEPTH) ** 0.25
BETA = (8 * DEPTH) ** -0.25
EPS = 1e-6

kernel_name = "hybrid_headgroup_deepnorm_moe_trunk"

def layer_norm(x, g, b):
    xf = x.astype(jnp.float32)
    mu = jnp.mean(xf, -1, keepdims=True)
    var = jnp.mean(jnp.square(xf - mu), -1, keepdims=True)
    y = (xf - mu) * lax.rsqrt(var + EPS)
    return (y * g.astype(jnp.float32) + b.astype(jnp.float32)).astype(x.dtype)

def rms_norm(x, g):
    xf = x.astype(jnp.float32)
    y = xf * lax.rsqrt(jnp.mean(jnp.square(xf), -1, keepdims=True) + EPS)
    return (y * g.astype(jnp.float32)).astype(x.dtype)

def apply_rope(t, cos, sin):
    half = t.shape[-1] // 2
    t1, t2 = t[..., :half], t[..., half:]
    return jnp.concatenate([t1 * cos - t2 * sin, t2 * cos + t1 * sin], axis=-1)

def chunked_spatial_gating(za, v_norm_g, w_s, b_s):
    bsz, s_len, _ = za.shape
    z = jax.nn.gelu(za)
    u, v = jnp.split(z, 2, axis=-1)
    v = rms_norm(v, v_norm_g)
    n_chunks = s_len // CHUNK
    v = v.reshape(bsz, n_chunks, CHUNK, A_HEADS, A_HEAD_DIM)
    causal = jnp.tril(jnp.ones((CHUNK, CHUNK), dtype=bool))
    w = jnp.where(causal[None], w_s, 0)
    mixed = jnp.einsum('hts,bcshd->bcthd', w, v) + b_s.T[None, None, :, :, None]
    return u * mixed.reshape(bsz, s_len, A_WIDTH)

def latent_attention(zb, cos, sin, q_norm_g, w_uq, kv_norm_g, w_ukv):
    bsz, s_len, _ = zb.shape
    c_q = rms_norm(zb[..., :Q_LORA], q_norm_g)
    c_kv = rms_norm(zb[..., Q_LORA:Q_LORA + KV_LORA], kv_norm_g)
    k_rope = apply_rope(zb[..., Q_LORA + KV_LORA:], cos, sin)
    q = (c_q @ w_uq).reshape(bsz, s_len, MLA_HEADS, MLA_NOPE + MLA_ROPE)
    q_nope = q[..., :MLA_NOPE]
    q_rope = apply_rope(q[..., MLA_NOPE:], cos[:, :, None, :], sin[:, :, None, :])
    kv = (c_kv @ w_ukv).reshape(bsz, s_len, MLA_HEADS, MLA_NOPE + MLA_V)
    k_nope, v = kv[..., :MLA_NOPE], kv[..., MLA_NOPE:]
    scale = (MLA_NOPE + MLA_ROPE) ** -0.5
    n_blocks = s_len // Q_BLOCK
    key_idx = jnp.arange(s_len)

    def to_blocks(t):
        return jnp.moveaxis(t.reshape(bsz, n_blocks, Q_BLOCK, *t.shape[2:]), 1, 0)

    def attend(args):
        qn, qr, blk = args
        s = (jnp.einsum('bqhd,bkhd->bhqk', qn, k_nope)
             + jnp.einsum('bqhr,bkr->bhqk', qr, k_rope)).astype(jnp.float32) * scale
        q_idx = blk * Q_BLOCK + jnp.arange(Q_BLOCK)
        s = jnp.where(key_idx[None, :] <= q_idx[:, None], s, -jnp.inf)
        p = jax.nn.softmax(s, axis=-1).astype(v.dtype)
        return jnp.einsum('bhqk,bkhd->bqhd', p, v)

    o = lax.map(attend, (to_blocks(q_nope), to_blocks(q_rope), jnp.arange(n_blocks)))
    return jnp.moveaxis(o, 0, 1).reshape(bsz, s_len, MLA_WIDTH)

def short_gated_conv(zc, conv_w):
    b_gate, c_gate, h = jnp.split(zc, 3, axis=-1)
    y = lax.conv_general_dilated(
        c_gate * h, conv_w[:, None, :], window_strides=(1,), padding=[(CONV_W - 1, 0)],
        dimension_numbers=('NWC', 'WIO', 'NWC'), feature_group_count=C_WIDTH)
    return b_gate * y

def multiscale_pool(zd, pool_w, pool_scale):
    bsz, s_len, _ = zd.shape
    zf = zd.astype(jnp.float32)
    cs = jnp.concatenate([jnp.zeros((bsz, 1, D_WIDTH), jnp.float32), jnp.cumsum(zf, axis=1)], axis=1)
    t1 = jnp.arange(1, s_len + 1)
    outs = []
    for g, w in enumerate(POOL_WINDOWS):
        cs_g = cs[..., g * D_GROUP:(g + 1) * D_GROUP]
        lo = jnp.maximum(t1 - w, 0)
        win_sum = cs_g[:, 1:] - jnp.take(cs_g, lo, axis=1)
        count = jnp.minimum(t1, w).astype(jnp.float32)[None, :, None]
        outs.append(win_sum / count - zf[..., g * D_GROUP:(g + 1) * D_GROUP])
    pooled = jnp.stack(outs, axis=2).astype(zd.dtype)
    y = jnp.einsum('bsgc,gcd->bsgd', pooled, pool_w).reshape(bsz, s_len, D_WIDTH)
    return y * pool_scale

def hybrid_mixer(x, cos, sin, w_in, gmlp_v_norm_g, gmlp_w_s, gmlp_b_s, mla_q_norm_g, mla_w_uq,
                 mla_kv_norm_g, mla_w_ukv, conv_w, pool_w, pool_scale, w_out):
    z = x @ w_in
    za, zb, zc, zd = jnp.split(z, [P_A, P_A + P_B, P_A + P_B + P_C], axis=-1)
    ya = chunked_spatial_gating(za, gmlp_v_norm_g, gmlp_w_s, gmlp_b_s)
    yb = latent_attention(zb, cos, sin, mla_q_norm_g, mla_w_uq, mla_kv_norm_g, mla_w_ukv)
    yc = short_gated_conv(zc, conv_w)
    yd = multiscale_pool(zd, pool_w, pool_scale)
    y = jnp.concatenate([ya, yb, yc, yd], axis=-1)
    return y @ w_out

def memory_cross_attention(x, mem, wq, wk, wv, wo):
    bsz, s_len, _ = x.shape
    q = (x @ wq).reshape(bsz, s_len, X_HEADS, X_HEAD_DIM)
    k = (mem @ wk).reshape(bsz, -1, X_HEADS, X_HEAD_DIM)
    v = (mem @ wv).reshape(bsz, -1, X_HEADS, X_HEAD_DIM)
    s = jnp.einsum('bqhd,bkhd->bhqk', q, k).astype(jnp.float32) * (X_HEAD_DIM ** -0.5)
    p = jax.nn.softmax(s, axis=-1).astype(v.dtype)
    o = jnp.einsum('bhqk,bkhd->bqhd', p, v).reshape(bsz, s_len, D_MODEL)
    return o @ wo

def route_gates(xt, router_w, router_b):
    n_tok = xt.shape[0]
    scores = jax.nn.sigmoid((xt @ router_w).astype(jnp.float32))
    sel = scores + router_b.astype(jnp.float32)
    group_score = jnp.sum(lax.top_k(sel.reshape(n_tok, N_GROUPS, EXPERTS_PER_GROUP), TOP_K)[0], axis=-1)
    best_group = jnp.argmax(group_score, axis=-1)
    in_group = (jnp.arange(N_EXPERTS) // EXPERTS_PER_GROUP)[None, :] == best_group[:, None]
    _, idx = lax.top_k(jnp.where(in_group, sel, -jnp.inf), TOP_K)
    w = jnp.take_along_axis(scores, idx, axis=-1)
    w = w / jnp.sum(w, axis=-1, keepdims=True)
    return jnp.sum(jax.nn.one_hot(idx, N_EXPERTS, dtype=jnp.float32) * w[..., None], axis=1)

def grouped_moe(x, router_w, router_b, w_gate, w_up, w_down):
    bsz, s_len, d = x.shape
    xt = x.reshape(-1, d)
    gates = route_gates(xt, router_w, router_b).astype(x.dtype)
    out = jnp.zeros_like(xt)
    for e in range(N_EXPERTS):
        h = jax.nn.silu(xt @ w_gate[e]) * (xt @ w_up[e])
        out = out + gates[:, e:e + 1] * (h @ w_down[e])
    return out.reshape(bsz, s_len, d)

def setup_inputs(seed: int = 0) -> dict:
    key = jax.random.key(seed)
    keys = iter(jax.random.split(key, 40))
    L = DEPTH

    def nrm(shape, scale):
        return jax.random.normal(next(keys), shape, jnp.float32) * scale

    def gain(shape):
        return 1.0 + 0.05 * jax.random.normal(next(keys), shape, jnp.float32)

    x = nrm((BATCH, SEQ, D_MODEL), 1.0)
    mem = nrm((BATCH, MEM_LEN, D_MODEL), 1.0)
    positions = (jax.random.randint(next(keys), (BATCH, 1), 0, SEQ, dtype=jnp.int32)
                 + jnp.arange(SEQ, dtype=jnp.int32)[None, :])
    return {
        'x': x,
        'mem': mem,
        'positions': positions,
        'w_in': nrm((L, D_MODEL, P_IN), D_MODEL ** -0.5),
        'gmlp_v_norm_g': gain((L, A_WIDTH)),
        'gmlp_w_s': nrm((L, A_HEADS, CHUNK, CHUNK), CHUNK ** -0.5),
        'gmlp_b_s': 1.0 + 0.1 * nrm((L, A_HEADS, CHUNK), 1.0),
        'mla_q_norm_g': gain((L, Q_LORA)),
        'mla_w_uq': nrm((L, Q_LORA, MLA_HEADS * (MLA_NOPE + MLA_ROPE)), Q_LORA ** -0.5),
        'mla_kv_norm_g': gain((L, KV_LORA)),
        'mla_w_ukv': nrm((L, KV_LORA, MLA_HEADS * (MLA_NOPE + MLA_V)), KV_LORA ** -0.5),
        'conv_w': nrm((L, CONV_W, C_WIDTH), CONV_W ** -0.5),
        'pool_w': nrm((L, len(POOL_WINDOWS), D_GROUP, D_GROUP), D_GROUP ** -0.5),
        'pool_scale': gain((L, D_WIDTH)),
        'w_out': nrm((L, MIX_WIDTH, D_MODEL), BETA * MIX_WIDTH ** -0.5),
        'ln1_g': gain((L, D_MODEL)),
        'ln1_b': nrm((L, D_MODEL), 0.02),
        'xattn_wq': nrm((L, D_MODEL, D_MODEL), D_MODEL ** -0.5),
        'xattn_wk': nrm((L, D_MODEL, D_MODEL), D_MODEL ** -0.5),
        'xattn_wv': nrm((L, D_MODEL, D_MODEL), BETA * D_MODEL ** -0.5),
        'xattn_wo': nrm((L, D_MODEL, D_MODEL), BETA * D_MODEL ** -0.5),
        'ln2_g': gain((L, D_MODEL)),
        'ln2_b': nrm((L, D_MODEL), 0.02),
        'router_w': nrm((D_MODEL, N_EXPERTS), D_MODEL ** -0.5),
        'router_b': nrm((N_EXPERTS,), 0.01),
        'moe_w_gate': nrm((L, N_EXPERTS, D_MODEL, D_FF_EXPERT), D_MODEL ** -0.5),
        'moe_w_up': nrm((L, N_EXPERTS, D_MODEL, D_FF_EXPERT), D_MODEL ** -0.5),
        'moe_w_down': nrm((L, N_EXPERTS, D_FF_EXPERT, D_MODEL), BETA * D_FF_EXPERT ** -0.5),
        'ln3_g': gain((L, D_MODEL)),
        'ln3_b': nrm((L, D_MODEL), 0.02),
    }

def reference(x, mem, positions, w_in, gmlp_v_norm_g, gmlp_w_s, gmlp_b_s, mla_q_norm_g, mla_w_uq,
              mla_kv_norm_g, mla_w_ukv, conv_w, pool_w, pool_scale, w_out, ln1_g, ln1_b,
              xattn_wq, xattn_wk, xattn_wv, xattn_wo, ln2_g, ln2_b, router_w, router_b,
              moe_w_gate, moe_w_up, moe_w_down, ln3_g, ln3_b):
    inv_freq = ROPE_BASE ** (-jnp.arange(0, MLA_ROPE, 2, dtype=jnp.float32) / MLA_ROPE)
    ang = positions.astype(jnp.float32)[..., None] * inv_freq
    cos = jnp.cos(ang).astype(x.dtype)
    sin = jnp.sin(ang).astype(x.dtype)
    for l in range(DEPTH):
        h = hybrid_mixer(x, cos, sin, w_in[l], gmlp_v_norm_g[l], gmlp_w_s[l], gmlp_b_s[l],
                         mla_q_norm_g[l], mla_w_uq[l], mla_kv_norm_g[l], mla_w_ukv[l],
                         conv_w[l], pool_w[l], pool_scale[l], w_out[l])
        x = layer_norm(ALPHA * x + h, ln1_g[l], ln1_b[l])
        h = memory_cross_attention(x, mem, xattn_wq[l], xattn_wk[l], xattn_wv[l], xattn_wo[l])
        x = layer_norm(ALPHA * x + h, ln2_g[l], ln2_b[l])
        h = grouped_moe(x, router_w, router_b, moe_w_gate[l], moe_w_up[l], moe_w_down[l])
        x = layer_norm(ALPHA * x + h, ln3_g[l], ln3_b[l])
    return x


_drawn_inputs = setup_inputs


def setup_inputs(seed=0):
    import zlib

    import numpy as np

    out = dict(_drawn_inputs(seed))
    spreads = {}
    factors = {'gmlp_v_norm_g': 3.59, 'mla_q_norm_g': 6.28, 'mla_kv_norm_g': 5.335}
    for name, (base, spread) in spreads.items():
        noise = np.random.default_rng([zlib.crc32(name.encode()), seed]).standard_normal(out[name].shape)
        drawn = base * np.exp(spread * noise) if base else spread * noise
        out[name] = __import__('jax').numpy.asarray(drawn.astype(out[name].dtype))
    for name, factor in factors.items():
        out[name] = (out[name] * factor).astype(out[name].dtype)
    return out
```

```python
from contextlib import ExitStack

import numpy as np

import concourse.bass as bass
from concourse import mybir

F32 = mybir.dt.float32
F32R = mybir.dt.float32r
BF16 = mybir.dt.bfloat16
I32 = mybir.dt.int32
ALU = mybir.AluOpType
ACT = mybir.ActivationFunctionType
AX_X = mybir.AxisListType.X

P = 128
CHUNK = 128
A_HEADS, A_DIM = 4, 64
MLA_HEADS, NOPE, ROPE, MLA_V = 8, 64, 32, 64
ROPE_BASE = 10000.0
POOL_WINDOWS = (2, 4, 8, 16)
PAD = max(POOL_WINDOWS)
CONV_W = 3
X_HEADS = 4
N_GROUPS, PER_GROUP = 4, 4
EPS = 1e-6
MLA_SCALE = float(NOPE + ROPE) ** -0.5
GELU_CUBIC = 0.044715
GELU_SCALE = float(np.sqrt(2.0 / np.pi))
MASKED = -1e30
TWO_PI = 2.0 * np.pi
TURN_HI = float(np.float32(6.28125))
TURN_MID = float(np.float32(np.round((TWO_PI - 6.28125) * 2.0**21) / 2.0**21))
TURN_LO = float(np.float32(TWO_PI - TURN_HI - TURN_MID))
ROUND_MAGIC = 1.5 * 2.0**23
PI_BELOW = 3.1415925

RAW_SLOTS = 6
SPLIT_SLOTS = 2

IN_UNITS = ["cq", "ckv", "v", "u", "b", "c", "h", "d"]
U_OUT = len(IN_UNITS)
OUT_CHUNKS = [(6, 2), (0, 2), (8, 2), (2, 2), (4, 1), (5, 1)]
U_K = U_OUT + len(OUT_CHUNKS)
U_V = U_K + 4
U_Q = U_V + 4
U_O = U_Q + 4
U_MOE = U_O + 4


def ring_jobs():
    jobs = [(f"xa{i}", "dve") for i in range(4)]
    jobs += [("cq", "act"), ("ckv", "dve"), ("v", "act"), ("ssq", "dve"), ("ssk", "dve"), ("u", "act"),
             ("rb0", "dve"), ("b", "act")]
    jobs += [("qn0", "act"), ("qn1", "act"), ("qr", "dve"), ("qrs", "dve"), ("kn0", "act"), ("kn1", "act"),
             ("vv0", "act"), ("vv1", "act")]
    jobs += [("s0", "act"), ("s1", "act"), ("c", "act"), ("s2", "act"), ("s3", "act"), ("wst", "act"), ("h", "act"),
             ("pt0", "act"), ("pt1", "act"), ("s4", "act"), ("s5", "act"), ("d", "act"),
             ("pv0", "dve"), ("mix", "dve"), ("pt2", "act"), ("pt3", "act"), ("s6", "act"), ("s7", "act"),
             ("pv1", "dve"), ("pt4", "act"), ("pt5", "act"), ("yd", "dve"), ("pv2", "dve"), ("pt6", "act"),
             ("pt7", "act"), ("pv3", "dve")]
    jobs += [(f"xk{i}", "act") for i in range(4)]
    jobs += [(f"xb{i}", "dve") for i in range(4)]
    jobs += [(f"xq{i}", "act") for i in range(4)]
    jobs += [(f"cs{i}", "act") for i in range(4)]
    for i in range(4):
        jobs += [(f"cpt{i}", "act"), (f"cpv{i}", "act")]
    jobs += [(f"xc{i}", "dve") for i in range(4)]
    jobs += [("rt0", "dve"), ("rt1", "dve")]
    jobs += [(f"gb{i}", "act") for i in range(8)]
    return jobs


def hybrid_trunk_kernel(nc, x, mem, positions, w_in, gmlp_v_norm_g, gmlp_w_s, gmlp_b_s, mla_q_norm_g,
                        mla_w_uq, mla_kv_norm_g, mla_w_ukv, conv_w, pool_w, pool_scale, w_out, ln1_g,
                        ln1_b, xattn_wq, xattn_wk, xattn_wv, xattn_wo, ln2_g, ln2_b, router_w, router_b,
                        moe_w_gate, moe_w_up, moe_w_down, ln3_g, ln3_b, rope_freq, rope_sign, pool_inv, out):
    _, SEQ, D = x.shape
    DEPTH = w_in.shape[0]
    E = router_w.shape[1]
    T = SEQ // P
    DC = D // P
    MIX = w_out.shape[1]
    YC = MIX // P
    FF = moe_w_gate.shape[3]
    QL = mla_w_uq.shape[1]
    ALPHA = float((2 * DEPTH) ** 0.25)
    assert T == 2 and DC == 8 and YC == 10 and FF == 256 and E == 16 and QL == 256

    UNITS = U_MOE + 3 * E
    JOBS = ring_jobs()
    MISC = len(JOBS)
    while MISC % 4:
        raise AssertionError(f"{MISC} ring jobs: the banks must come round with the layer")
    INDEX = {name: i for i, (name, _) in enumerate(JOBS)}
    unit_jobs = set(IN_UNITS) | {f"xk{i}" for i in range(4)} | {f"xq{i}" for i in range(4)}
    ACT_LAYER = sum(by == "act" for _, by in JOBS)
    DVE_LAYER = sum(by == "dve" for _, by in JOBS) + 2 * E
    MISC_LAYER = sum(n not in unit_jobs for n, _ in JOBS)
    PRO = 4

    def emptied(name, l):
        i = INDEX[name]
        by = JOBS[i][1]
        n = sum(b == by for _, b in JOBS[:i + 1])
        return (l * ACT_LAYER + n) if by == "act" else (l * DVE_LAYER + n + PRO)

    def misc_done(name, l):
        return l * MISC_LAYER + sum(n not in unit_jobs for n, _ in JOBS[:INDEX[name] + 1]) + PRO

    def used(u, l):
        return l * UNITS + (u + 1 + SPLIT_SLOTS)

    def split(u, l):
        return l * UNITS + (u + 1 + RAW_SLOTS)

    with ExitStack() as ctx:
        def sb(name, shape, dt=F32):
            return ctx.enter_context(nc.sbuf_tensor(name, shape, dt))

        def sem(name):
            return ctx.enter_context(nc.semaphore(name))

        raw = sb("raw", [P, RAW_SLOTS, 2048])
        w_hi = sb("w_hi", [P, SPLIT_SLOTS, 2048], F32R)
        w_lo = sb("w_lo", [P, SPLIT_SLOTS, 2048], F32R)
        X = sb("X", [P, T, D])
        x_hi = sb("x_hi", [P, DC, SEQ], F32R)
        x_lo = sb("x_lo", [P, DC, SEQ], F32R)
        memT = sb("memT", [P, DC, SEQ])
        y_hi = sb("y_hi", [P, YC, SEQ], F32R)
        y_lo = sb("y_lo", [P, YC, SEQ], F32R)
        ln_w = sb("ln_w", [P, 2, D])
        wukv = sb("wukv", [P, MLA_HEADS * (NOPE + MLA_V)])
        ws = sb("ws", [P, A_HEADS, CHUNK])
        wsT = sb("wsT", [P, A_HEADS, CHUNK])
        bs = sb("bs", [P, 2, CHUNK])
        vg = sb("vg", [P, 256])
        pw = sb("pw", [P, 2, 64])
        cw = sb("cw", [P, 2, CONV_W])
        psc = sb("psc", [P, 2])
        qg = sb("qg", [P, 3])
        rope_cos = sb("rope_cos", [P, SEQ])
        rope_sin = sb("rope_sin", [P, SEQ])
        freq = sb("freq", [P, 2])
        ident = sb("ident", [P, P])
        causal = sb("causal", [P, P])
        ones = sb("ones", [P, 2])
        minus_half = sb("minus_half", [P, 4])
        pinv = sb("pinv", [P, 2, PAD + 1])
        rw_hi = sb("rw_hi", [P, DC, E], F32R)
        rw_lo = sb("rw_lo", [P, DC, E], F32R)
        rb = sb("rb", [P, E])
        ms = sb("ms", [P, 4])
        rs = sb("rs", [P, 4])
        vms = sb("vms", [P, 2])
        vrs = sb("vrs", [P, 2])
        smax = sb("smax", [P, 8, 2])
        ssum = sb("ssum", [P, 8, 2])
        srec = sb("srec", [P, 8, 2])
        bn = sb("bn", [P, T, 2, 6])
        mv = sb("mv", [P, T, 2])
        lv = sb("lv", [P, T])
        lr = sb("lr", [P, T])
        gates = sb("gates", [P, T, E])
        before = sb("before", [P, P])
        slots = sb("slots", [P, P], BF16)
        place = sb("place", [P, T, N_GROUPS])
        slot_gates = sb("slot_gates", [P, E])
        fits = sb("fits", [P, 1], I32)
        ARENA = -(-nc.sbuf_base // 32) * 32
        arena = sb("arena", [P, 11632])

        def rounded(name, off, *shape):
            return nc.alloc_sbuf_tensor_at(name, [P, *shape], F32R, offset=ARENA + 4 * off)

        def at(off, *shape):
            n = int(np.prod(shape))
            v = arena[:, off:off + n]
            if len(shape) == 2:
                v = v.rearrange("p (a b) -> p a b", a=shape[0])
            return v

        cT = at(0, 4, SEQ)
        sq = at(1024, 3, SEQ)
        cn = at(1792, 3, SEQ)
        probs = at(1024, 4, 384)
        probsT = at(0, 2, 384)
        qn = at(2560, 4, SEQ)
        qr = at(3584, 2, SEQ)
        kn = at(4096, 4, SEQ)
        kr = at(5120, SEQ)
        vv = at(5376, T, 512)
        vz = at(6400, T, 256)
        gt = at(6912, 2, 256)
        th = at(7424, 2, 256)
        uz = at(7936, 2, 256)
        zb = at(8448, 2, 256)
        zc = at(8960, 2, 256)
        rtmp = zc
        chp = at(9472, 2, CONV_W - 1 + SEQ)
        pa = at(10000, 2, PAD + SEQ)
        pb_ = at(10544, 2, PAD + SEQ)
        pc = at(11088, 2, PAD + SEQ)
        wuq_in = at(10096, 2, MLA_HEADS * (NOPE + ROPE))
        wuq = [at(4096 + 1280 * c, 1024) for c in range(2)]
        kT = at(0, DC, SEQ)
        xv = at(2048, T, D)
        qT = at(4096, DC, SEQ)
        xprobs = at(6144, 4, 512)
        xprobsT = at(8192, 2, 512)
        gbc = at(0, E, SEQ)
        m_th = at(4096, 512)
        m_t = at(4608, 2, 512)
        rt = at(5632, 7, T * E).rearrange("p a (t e) -> p a t e", t=T)
        w_third = [rounded("w_third_hi", 6000, 2048), rounded("w_third_lo", 8048, 2048)]
        xn_hi = rounded("xn_hi", 0, T, DC, P)
        xn_lo = rounded("xn_lo", 2048, T, DC, P)
        s_t = at(4096, 2, FF)
        s_th = wsT[:].rearrange("p a b -> p (a b)").rearrange("p (a b) -> p a b", a=2)
        to_token = rounded("to_token", 4608, N_GROUPS, SEQ)
        mem_in = at(0, T, D)
        ang = at(2048, 4, SEQ)
        pos_i = at(3072, SEQ)
        rwraw = at(3328, DC, E)

        ring = ctx.enter_context(nc.psum_tensor("ring", [P, 4, 512], F32))
        quad = ctx.enter_context(nc.psum_tensor("quad", [P, 4, 512], F32))

        def bank(name):
            return ring[:, INDEX[name] % 4, :]

        def to_slot(t):
            return (y_hi, y_lo)[t][:, 8:10, :].rearrange("p a b -> p (a b)")

        def bank2(name):
            return bank(name).rearrange("p (a b) -> p a b", a=2)

        raw_full = [sem(f"raw_full{i}") for i in range(RAW_SLOTS)]
        hi_done = sem("hi_done")
        split_done = sem("split_done")
        unit_used = sem("unit_used")
        misc_ready = sem("misc_ready")
        act_emptied = sem("act_emptied")
        dve_emptied = sem("dve_emptied")
        quad_free = sem("quad_free")
        quad_v = sem("quad_v")
        ident_ready = sem("ident_ready")
        sp_passed = sem("sp_passed")
        pe_passed = sem("pe_passed")
        act_passed = sem("act_passed")
        xhi_done = sem("xhi_done")
        start_full = sem("start_full")
        pre_full = sem("pre_full")
        small_full = sem("small_full")
        ln_full = sem("ln_full")
        ln_read = sem("ln_read")
        ln_var = sem("ln_var")
        ln_rstd = sem("ln_rstd")
        x_ready = sem("x_ready")
        ws_masked = sem("ws_masked")
        sq_ready = sem("sq_ready")
        wuq_ready = sem("wuq_ready")
        ms_ready = sem("ms_ready")
        rs_ready = sem("rs_ready")
        cn_ready = sem("cn_ready")
        vms_ready = sem("vms_ready")
        vrs_ready = sem("vrs_ready")
        gelu_arg = sem("gelu_arg")
        gelu_tanh = sem("gelu_tanh")
        v_ready = sem("v_ready")
        rope_ready = sem("rope_ready")
        max_ready = sem("max_ready")
        probs_ready = sem("probs_ready")
        pooled = sem("pooled")
        y_ready = sem("y_ready")
        mem_split = sem("mem_split")
        memhl = sem("memhl")
        xmax_ready = sem("xmax_ready")
        xprobs_ready = sem("xprobs_ready")
        logit = sem("logit")
        sig_exp = sem("sig_exp")
        gates_ready = sem("gates_ready")
        xn_hi_done = sem("xn_hi_done")
        xn_lo_done = sem("xn_lo_done")
        member_ready = sem("member_ready")
        placed = sem("placed")
        fits_ready = sem("fits_ready")
        slots_ready = sem("slots_ready")
        gathered = sem("gathered")
        gath_hi = sem("gath_hi")
        gath_lo = sem("gath_lo")
        slot_gated = sem("slot_gated")
        to_token_done = sem("to_token_done")
        to_token_moved = sem("to_token_moved")
        turned = sem("turned")
        turned_hi = sem("turned_hi")
        out_hi = sem("out_hi")
        out_split = sem("out_split")
        moe_done = sem("moe_done")
        moe_tanh = sem("moe_tanh")
        h_ready = sem("h_ready")
        rope_arg = sem("rope_arg")
        rope_sined = sem("rope_sined")
        rwhi = sem("rwhi")
        stored = sem("stored")

        block = ctx.enter_context(nc.Block())

        STEPS = (E - 2) // 2

        def gate_unit(k):
            return U_MOE + (2 * k if k < 2 else 3 * k - 2)

        def up_unit(k):
            return U_MOE + (1 if k == 0 else 3 * k)

        def down_unit(k):
            return U_MOE + 3 * k + 5 if k < E - 2 else UNITS - E + k

        def slot(u):
            return u % SPLIT_SLOTS if u < U_MOE else (u - U_MOE + 2) % 3

        def slot_before(u):
            return u - (SPLIT_SLOTS if u < U_MOE else 3)

        def unit_slot(u, part, n):
            k = slot(u)
            return (w_third[part][:, 0:n] if k == 2 else (w_hi, w_lo)[part][:, k, 0:n])

        KV_COLS = 192
        KV_PIECES = ((slice(0, 160), slice(0, 160)), (slice(160, 176), slice(144, 160)), (slice(176, 192), slice(128, 144)))

        def kv_views(dst):
            return (dst[:, 1 % SPLIT_SLOTS, 0:DC * KV_COLS].rearrange("p (k n) -> p k n", k=DC),
                    raw[:, 1 % RAW_SLOTS, 0:DC * 160].rearrange("p (k n) -> p k n", k=DC))

        @block.sync
        def _(sp):
            def load(u, l, src, shape, i=0):
                sp.wait_ge(split_done, split(u, l) - RAW_SLOTS + i)
                sp.sem_inc(sp_passed, 1)
                n = int(np.prod(shape))
                dst = raw[:, u % RAW_SLOTS, 0:n].rearrange("p (a b) -> p a b", a=shape[0])
                sp.dma_start(dst, src).then_inc(raw_full[u % RAW_SLOTS], 16)

            def by_columns(w, c0, n):
                return w[:, c0:c0 + n].rearrange("(p c) n -> p c n", c=DC)

            def expert(l, e, what, u, i):
                if what == "d":
                    load(u, l, moe_w_down[l, e].rearrange("(c p) n -> p c n", p=P), (2, D), i)
                else:
                    w = moe_w_gate if what == "g" else moe_w_up
                    load(u, l, w[l, e].rearrange("(p c) n -> p c n", c=DC), (DC, FF), i)

            with sp.Fori(0, DEPTH) as l:
                first = {"u": 0, "v": 256, "cq": 512, "ckv": 768, "b": 928, "c": 1184, "h": 1440, "d": 1696}
                for u, name in enumerate(IN_UNITS):
                    n = 160 if name == "ckv" else 256
                    load(u, l, by_columns(w_in[l], first[name], n), (DC, n))
                for i, (c0, n) in enumerate(OUT_CHUNKS):
                    src = w_out[l, c0 * P:(c0 + n) * P, :].rearrange("(c p) n -> p c n", p=P)
                    load(U_OUT + i, l, src, (n, D))
                for i in range(4):
                    load(U_K + i, l, by_columns(xattn_wk[l], 256 * i, 256), (DC, 256))
                for i in range(4):
                    load(U_V + i, l, xattn_wv[l].rearrange("(p c) n -> p c n", c=DC)[:, 2 * i:2 * i + 2, :], (2, D))
                for i in range(4):
                    load(U_Q + i, l, by_columns(xattn_wq[l], 256 * i, 256), (DC, 256))
                for i in range(4):
                    src = xattn_wo[l, 2 * i * P:(2 * i + 2) * P, :].rearrange("(c p) n -> p c n", p=P)
                    load(U_O + i, l, src, (2, D))
                for k in range(2):
                    expert(l, k, "g", gate_unit(k), 0)
                    expert(l, k, "u", up_unit(k), 0)
                with sp.Fori(0, STEPS) as i:
                    for k in (2, 3):
                        expert(l, i * 2 + k, "g", gate_unit(k), i * 6)
                        expert(l, i * 2 + (k - 2), "d", down_unit(k - 2), i * 6)
                        expert(l, i * 2 + k, "u", up_unit(k), i * 6)
                for k in (E - 2, E - 1):
                    expert(l, k, "d", down_unit(k), 0)
            sp.wait_ge(x_ready, T + 3 * T * DEPTH)
            sp.dma_start(out[0].rearrange("(t p) d -> p t d", p=P), X[:]).then_inc(stored, 16)
            sp.wait_ge(stored, 16)

        @block.gpsimd
        def _(pool):
            pool.dma_start(X[:], x[0].rearrange("(t p) d -> p t d", p=P)).then_inc(start_full, 16)
            pool.dma_start(mem_in, mem[0].rearrange("(t p) d -> p t d", p=P)).then_inc(start_full, 16)
            with nc.allow_non_contiguous_dma(reason="small vectors, one element a partition"):
                pool.dma_start(pos_i.bitcast(I32), positions[0].partition_broadcast(P)).then_inc(pre_full, 16)
                pool.dma_start(freq[:, 0:1], rope_freq.rearrange("(p a) -> p a", a=1)).then_inc(pre_full, 16)
                pool.dma_start(freq[:, 1:2], rope_sign.rearrange("(p a) -> p a", a=1)).then_inc(pre_full, 16)
                pool.dma_start(pinv[:], pool_inv).then_inc(pre_full, 16)
                pool.dma_start(rwraw, router_w.rearrange("(p c) e -> p c e", c=DC)).then_inc(pre_full, 16)
                pool.dma_start(rb[:], router_b.partition_broadcast(P)).then_inc(pre_full, 16)
            nc.gpsimd.memset(ident[:], 0.0)
            nc.gpsimd.memset(causal[:], 0.0)
            nc.gpsimd.memset(minus_half[:], -0.5)
            nc.gpsimd.memset(ones[:], 1.0)
            nc.gpsimd.memset(before[:], 1.0)
            pool.drain()
            nc.gpsimd.affine_select(out=ident[:], in_=ident[:], compare_op=ALU.not_equal, fill=1.0, base=0,
                                    pattern=[[-1, P]], channel_multiplier=1)
            nc.gpsimd.affine_select(out=causal[:], in_=causal[:], compare_op=ALU.is_ge, fill=MASKED, base=0,
                                    pattern=[[-1, P]], channel_multiplier=1)
            nc.gpsimd.affine_select(out=before[:], in_=before[:], compare_op=ALU.is_gt, fill=0.0, base=0,
                                    pattern=[[1, P]], channel_multiplier=-1)
            nc.gpsimd.iota(slots[:], pattern=[[1, P]], base=0, channel_multiplier=0,
                           allow_small_or_imprecise_dtypes=True)
            pool.drain().then_inc(ident_ready, 1)

            for l in range(DEPTH):
                if l:
                    pool.wait_ge(unit_used, used(U_K - 1, l - 1))
                with nc.allow_non_contiguous_dma(reason="small vectors, one element a partition"):
                    small = [
                        (wuq_in, mla_w_uq[l].rearrange("(c p) n -> p c n", p=P)),
                        (wukv[:], mla_w_ukv[l]),
                        (ws[:], gmlp_w_s[l].rearrange("h t s -> t h s")),
                        (vg[:], gmlp_v_norm_g[l].partition_broadcast(P)),
                        (qg[:, 0:2], mla_q_norm_g[l].rearrange("(c p) -> p c", p=P)),
                        (qg[:, 2:3], mla_kv_norm_g[l].rearrange("(p a) -> p a", a=1)),
                        (psc[:], pool_scale[l].rearrange("(c p) -> p c", p=P)),
                    ]
                    small += [(cw[:, c, :], conv_w[l][:, c * P:(c + 1) * P].rearrange("k p -> p k")) for c in range(2)]
                    small += [(pw[64 * (g % 2):64 * (g % 2) + 64, g // 2, :], pool_w[l, g]) for g in range(4)]
                    small += [(bs[64 * (h % 2):64 * (h % 2) + 64, h // 2, :], gmlp_b_s[l, h].partition_broadcast(64))
                              for h in range(A_HEADS)]
                    for dst, src in small:
                        pool.dma_start(dst, src).then_inc(small_full, 16)
                SMALL = 16 * len(small)

                def load_ln(g, b, n):
                    if n:
                        pool.wait_ge(ln_read, 2 * T * n)
                    pool.dma_start(ln_w[:, 0, :], g.partition_broadcast(P)).then_inc(ln_full, 16)
                    pool.dma_start(ln_w[:, 1, :], b.partition_broadcast(P)).then_inc(ln_full, 16)

                def ln_power(n):
                    for t in range(T):
                        pool.wait_ge(ln_var, n * T + t + 1)
                        nc.gpsimd.tensor_tensor(lr[:, t:t + 1], lv[:, t:t + 1], minus_half[:, 0:1],
                                                ALU.pow).then_inc(ln_rstd, 1)

                load_ln(ln1_g[l], ln1_b[l], 3 * l)
                pool.wait_ge(small_full, SMALL * (l + 1))
                nc.gpsimd.affine_select(out=ws[:], in_=ws[:], compare_op=ALU.is_ge, fill=0.0, base=0,
                                        pattern=[[0, A_HEADS], [-1, CHUNK]],
                                        channel_multiplier=1).then_inc(ws_masked, 1)
                pool.wait_ge(ms_ready, l + 1)
                nc.gpsimd.tensor_tensor(rs[:], ms[:], minus_half[:], ALU.pow).then_inc(rs_ready, 1)
                pool.wait_ge(vms_ready, l + 1)
                nc.gpsimd.tensor_tensor(vrs[:], vms[:], minus_half[:, 0:2], ALU.pow).then_inc(vrs_ready, 1)
                ln_power(3 * l)
                load_ln(ln2_g[l], ln2_b[l], 3 * l + 1)
                ln_power(3 * l + 1)
                load_ln(ln3_g[l], ln3_b[l], 3 * l + 2)
                pool.wait_ge(xn_hi_done, l + 1)
                for t in range(T):
                    nc.gpsimd.tensor_tensor(xn_lo[:, t], X[:, t, :].rearrange("p (q c) -> p c q", c=DC),
                                            xn_hi[:, t].bitcast(F32), ALU.subtract)
                pool.drain().then_inc(xn_lo_done, 1)
                ln_power(3 * l + 2)

        SMALL_LAYER = 16 * 17
        DVE_AHEAD = DVE_LAYER - 2 * E + PRO

        @block.scalar
        def _(act):
            def hi(u, l, n, i=0):
                turns = l * (UNITS // RAW_SLOTS * 16) + (u // RAW_SLOTS + 1) * 16
                if not isinstance(i, int):
                    turns = turns + i * 16
                act.wait_ge(raw_full[u % RAW_SLOTS], turns)
                act.wait_ge(unit_used, used(slot_before(u), l) + (i * 6 if not isinstance(i, int) else 0))
                for a in range(2):
                    s = slice(a * n // 2, (a + 1) * n // 2)
                    nc.scalar.copy(unit_slot(u, 0, n)[:, s], raw[:, u % RAW_SLOTS, s]).then_inc(hi_done, 1)

            def hi_rotary(l):
                act.wait_ge(raw_full[1], l * (UNITS // RAW_SLOTS * 16) + 16)
                act.wait_ge(unit_used, used(1 - SPLIT_SLOTS, l))
                h, r = kv_views(w_hi)
                for d, sl in KV_PIECES:
                    nc.scalar.copy(h[:, :, d], r[:, :, sl])
                act.drain().then_inc(hi_done, 1)
                act.drain().then_inc(hi_done, 1)

            def move(name, l, dst, src, scale=1.0, unit=None):
                if unit is None:
                    act.wait_ge(misc_ready, misc_done(name, l))
                else:
                    act.wait_ge(unit_used, used(unit, l))
                nc.scalar.activation(dst, src, ACT.Copy, scale=scale).then_inc(act_emptied, 1)

            def x_high(name, l):
                for j in range(4):
                    act.wait_ge(misc_ready, misc_done(f"{name}{j}", l))
                    t, c = j // 2, 4 * (j % 2)
                    nc.scalar.copy(x_hi[:, c:c + 4, t * P:(t + 1) * P],
                                   bank(f"{name}{j}").rearrange("p (a b) -> p a b", a=4)).then_inc(xhi_done, 1)

            def exps(h, l):
                act.wait_ge(max_ready, l * MLA_HEADS + (h + 1))
                if h >= 4:
                    act.wait_ge(misc_ready, misc_done(f"pt{h - 4}", l))
                p = bank(f"s{h}")
                nc.scalar.activation(probs[:, h % 4, 0:128], p[:, 0:128], ACT.Exp, bias=smax[:, h, 0:1],
                                     accum_out=ssum[:, h, 0:1])
                nc.scalar.activation(probs[:, h % 4, 128:384], p[:, 128:384], ACT.Exp, bias=smax[:, h, 1:2],
                                     accum_out=ssum[:, h, 1:2])
                act.drain().then_inc(act_emptied, 1)

            def probs_t(h, l):
                if h >= 2:
                    act.wait_ge(misc_ready, misc_done(f"pv{h // 2 - 1}", l))
                move(f"pt{h}", l, probsT[:, h % 2, :], bank(f"pt{h}")[:, 0:384])

            def gelu_t(n, l):
                act.wait_ge(gelu_arg, l * 2 + (n + 1))
                nc.scalar.activation(th, gt, ACT.Tanh, scale=GELU_SCALE).then_inc(gelu_tanh, 1)

            act.wait_ge(rope_arg, 1)
            nc.scalar.activation(rope_cos[:], ang[:, 2, :], ACT.Sin)
            nc.scalar.activation(rope_sin[:], ang[:, 3, :], ACT.Sin)
            act.drain().then_inc(rope_sined, 1)
            act.wait_ge(pre_full, 16 * 6)
            nc.scalar.copy(rw_hi[:], rwraw).then_inc(rwhi, 1)

            NORMAL = 2048
            size = {1: DC * 160, U_OUT + 4: D, U_OUT + 5: D}

            with act.Fori(0, DEPTH) as l:
                def ahead(u):
                    hi(u + SPLIT_SLOTS, l, size.get(u + SPLIT_SLOTS, NORMAL))

                hi(0, l, NORMAL)
                hi_rotary(l)
                x_high("xa", l)
                move("cq", l, cT[:, 0:2, :], bank2("cq"), unit=0)
                ahead(0)
                ahead(1)
                move("v", l, vz, bank2("v"), unit=2)
                ahead(2)
                gelu_t(0, l)
                move("u", l, uz, bank2("u"), unit=3)
                ahead(3)
                gelu_t(1, l)
                move("b", l, zb, bank2("b"), unit=4)
                ahead(4)
                for i in range(2):
                    move(f"qn{i}", l, qn[:, 2 * i:2 * i + 2, :], bank2(f"qn{i}"), scale=MLA_SCALE)
                for i in range(2):
                    move(f"kn{i}", l, kn[:, 2 * i:2 * i + 2, :], bank2(f"kn{i}"))
                for i in range(2):
                    move(f"vv{i}", l, vv[:, i, :], bank(f"vv{i}"))
                exps(0, l)
                exps(1, l)
                move("c", l, zc, bank2("c"), unit=5)
                ahead(5)
                exps(2, l)
                exps(3, l)
                move("wst", l, wsT[:].rearrange("p a b -> p (a b)"), bank("wst"))
                move("h", l, chp[:, :, CONV_W - 1:], bank2("h"), unit=6)
                ahead(6)
                probs_t(0, l)
                probs_t(1, l)
                exps(4, l)
                exps(5, l)
                move("d", l, pa[:, :, PAD:], bank2("d"), unit=7)
                ahead(7)

                probs_t(2, l)
                probs_t(3, l)
                exps(6, l)
                exps(7, l)
                probs_t(4, l)
                probs_t(5, l)
                ahead(8)
                probs_t(6, l)
                probs_t(7, l)
                ahead(9)
                for u in range(10, 14):
                    ahead(u)
                act.wait_ge(unit_used, used(7, l))
                nc.scalar.copy(x_hi[:], memT[:]).then_inc(memhl, 1)
                for i in range(4):
                    move(f"xk{i}", l, kT[:, 2 * i:2 * i + 2, :], bank2(f"xk{i}"), unit=U_K + i)
                    ahead(U_K + i)
                for i in range(4):
                    ahead(U_V + i)
                act.wait_ge(unit_used, used(U_V + 3, l))
                for t in range(T):
                    for a in range(2):
                        last = nc.scalar.copy(xv[:, t, 512 * a:512 * a + 512], quad[:, 2 * t + a, :])
                last.then_inc(quad_v, 1)
                x_high("xb", l)
                for i in range(4):
                    move(f"xq{i}", l, qT[:, 2 * i:2 * i + 2, :], bank2(f"xq{i}"), scale=256.0 ** -0.5, unit=U_Q + i)
                    ahead(U_Q + i)
                for h in range(X_HEADS):
                    act.wait_ge(xmax_ready, l * X_HEADS + (h + 1))
                    for t in range(T):
                        nc.scalar.activation(xprobs[:, h, 256 * t:256 * t + 256],
                                             bank(f"cs{h}")[:, 256 * t:256 * t + 256], ACT.Exp,
                                             bias=smax[:, h, t:t + 1], accum_out=ssum[:, h, t:t + 1])
                    act.drain().then_inc(act_emptied, 1)
                for h in range(X_HEADS):
                    if h >= 2:
                        act.wait_ge(misc_ready, misc_done(f"cpv{h - 2}", l))
                    move(f"cpt{h}", l, xprobsT[:, h % 2, :], bank(f"cpt{h}"))
                    move(f"cpv{h}", l, qT[:, 2 * h:2 * h + 2, :], bank2(f"cpv{h}"))
                ahead(U_O)
                ahead(U_O + 1)
                act.wait_ge(y_ready, l * 11 + 11)
                for k in range(3):
                    hi(U_MOE + k, l, NORMAL)
                x_high("xc", l)
                act.wait_ge(logit, l + 1)
                nc.scalar.activation(rt[:, 1], rt[:, 0], ACT.Exp, scale=-1.0).then_inc(sig_exp, 1)
                for t in range(T):
                    last = nc.scalar.copy(xn_hi[:, t], X[:, t, :].rearrange("p (q c) -> p c q", c=DC))
                last.then_inc(xn_hi_done, 1)

                def tanh(dst, src, g_unit, i=0):
                    act.wait_ge(unit_used, used(g_unit, l) + i)
                    nc.scalar.activation(dst, src, ACT.Tanh, scale=0.5).then_inc(moe_tanh, 1)

                act.wait_ge(fits_ready, l + 1)
                act.sem_inc(act_passed, 1)
                with act.If(act.value_load(fits[0:1, 0:1], min_val=0, max_val=1)):
                    act.sem_inc(act_emptied, 8)

                    def gather_high(pair):
                        for r in range(4):
                            act.wait_ge(gathered, l * 8 + (4 * pair + r + 1))
                            nc.scalar.copy(x_hi[:, 2 * r:2 * r + 2, :],
                                           ring[:, r % 2, :].rearrange("p (a b) -> p a b", a=2)).then_inc(gath_hi, 1)

                    def turned_high(k):
                        act.wait_ge(turned, l * E + (k + 1))
                        nc.scalar.copy(y_hi[:, k % 2, :], ring[:, 1, FF:2 * FF]).then_inc(turned_hi, 1)

                    def out_high(g):
                        act.wait_ge(unit_used, used(down_unit(PER_GROUP * g + PER_GROUP - 1), l))
                        for a in range(2):
                            last = nc.scalar.copy(y_hi[:, 2 + 2 * a:4 + 2 * a, :],
                                                  ring[:, 2 + a, :].rearrange("p (a b) -> p a b", a=2))
                        last.then_inc(out_hi, 1)

                    gather_high(0)
                    act.wait_ge(to_token_done, l + 1)
                    for a in range(2):
                        last = nc.scalar.copy(to_token[:, 2 * a:2 * a + 2, :],
                                              ring[:, 2 + a, :].rearrange("p (a b) -> p a b", a=2))
                    last.then_inc(to_token_moved, 1)
                    tanh(s_th[:, 0, :], ring[:, 0, 0:FF], gate_unit(0))
                    for k in range(1, E):
                        if k == E // 2:
                            gather_high(1)
                        hi(up_unit(k), l, NORMAL)
                        tanh(s_th[:, k % 2, :], ring[:, 0, 0:FF], gate_unit(k))
                        turned_high(k - 1)
                        hi(up_unit(k) + 1, l, NORMAL)
                        if k >= 5 and k % PER_GROUP == 1:
                            out_high(k // PER_GROUP - 1)
                        hi(up_unit(k) + 2, l, NORMAL)
                    turned_high(E - 1)
                    out_high(N_GROUPS - 1)
                with act.Else():
                    act.wait_ge(xn_lo_done, l + 1)
                    for i in range(8):
                        move(f"gb{i}", l, gbc[:, 2 * i:2 * i + 2, :], bank2(f"gb{i}"), scale=0.5)
                    tanh(m_th, ring[:, 0, :], gate_unit(0))

                    def step(k, i, e):
                        hi(up_unit(k), l, NORMAL, i)
                        act.wait_ge(dve_emptied, l * DVE_LAYER + e * 2 + (DVE_AHEAD + 2 * k - 1))
                        tanh(m_th, ring[:, 2 * (k % 2), :], gate_unit(k), i if isinstance(i, int) else i * 6)
                        hi(up_unit(k) + 1, l, NORMAL, i)
                        hi(up_unit(k) + 2, l, NORMAL, i)

                    step(1, 0, 0)
                    with act.Fori(0, STEPS) as i:
                        step(2, i, i * 2)
                        step(3, i, i * 2)
                    act.sem_inc(gath_hi, 8)
                    act.sem_inc(to_token_moved, 1)
                    act.sem_inc(turned_hi, E)
                    act.sem_inc(out_hi, N_GROUPS)

        @block.vector
        def _(dve):
            def lo(u, l, n, i=0):
                for a in range(2):
                    c = l * (2 * UNITS) + (2 * u + a + 1)
                    dve.wait_ge(hi_done, c + i * 12 if not isinstance(i, int) else c)
                    s = slice(a * n // 2, (a + 1) * n // 2)
                    last = nc.vector.tensor_tensor(unit_slot(u, 1, n)[:, s], raw[:, u % RAW_SLOTS, s],
                                                   unit_slot(u, 0, n)[:, s].bitcast(F32), ALU.subtract)
                last.then_inc(split_done, 1)

            def lo_rotary(l):
                dve.wait_ge(hi_done, l * (2 * UNITS) + 4)
                w, r = kv_views(w_lo)
                h, _ = kv_views(w_hi)
                for d, sl in KV_PIECES:
                    nc.vector.tensor_tensor(w[:, :, d], r[:, :, sl], h[:, :, d].bitcast(F32), ALU.subtract)
                dve.drain().then_inc(split_done, 1)

            def x_low(name, l, n):
                for j in range(4):
                    dve.wait_ge(xhi_done, l * 12 + (4 * n + j + 1 + PRO * 0))
                    t, c = j // 2, 4 * (j % 2)
                    s = (slice(None), slice(c, c + 4), slice(t * P, (t + 1) * P))
                    nc.vector.tensor_tensor(x_lo[s], bank(f"{name}{j}").rearrange("p (a b) -> p a b", a=4),
                                            x_hi[s].bitcast(F32), ALU.subtract).then_inc(dve_emptied, 1)

            def split_y(c, n, src):
                nc.vector.tensor_copy(y_hi[:, c:c + n, :], src)
                dve.drain()
                nc.vector.tensor_tensor(y_lo[:, c:c + n, :], src, y_hi[:, c:c + n, :].bitcast(F32),
                                        ALU.subtract).then_inc(y_ready, 1)
                dve.drain()

            def gelu_poly(z):
                nc.vector.tensor_tensor(gt, z, z, ALU.mult)
                dve.drain()
                nc.vector.tensor_scalar(gt, gt, GELU_CUBIC, 1.0, ALU.mult, ALU.add)
                dve.drain()
                nc.vector.tensor_tensor(gt, gt, z, ALU.mult).then_inc(gelu_arg, 1)

            def gelu_end(z, n, l):
                dve.wait_ge(gelu_tanh, l * 2 + (n + 1))
                nc.vector.scalar_tensor_tensor(z, th, 1.0, z, ALU.add, ALU.mult)
                dve.drain()

            def head_max(h, l):
                dve.wait_ge(misc_ready, misc_done(f"s{h}", l))
                p = bank(f"s{h}")
                b = p[:, 0:384]
                diag = bass.AP(b.tensor, b.offset, [list(b.ap[0]), [256, 2], [1, 128]])
                mask = bass.AP(causal[:].tensor, 0, [list(causal[:].ap[0]), [0, 2], [1, 128]])
                nc.vector.tensor_tensor(diag, diag, mask, ALU.add)
                dve.drain()
                nc.vector.tensor_reduce(smax[:, h, 0:1], p[:, 0:128], AX_X, ALU.max, negate=True)
                nc.vector.tensor_reduce(smax[:, h, 1:2], p[:, 128:384], AX_X, ALU.max, negate=True)
                dve.drain().then_inc(max_ready, 1)

            def head_norm(h, l):
                dve.wait_ge(act_emptied, emptied(f"s{h}", l))
                nc.vector.reciprocal(srec[:, h, :], ssum[:, h, :])
                dve.drain()
                nc.vector.tensor_scalar(probs[:, h % 4, 0:128], probs[:, h % 4, 0:128], srec[:, h, 0:1], None, ALU.mult)
                nc.vector.tensor_scalar(probs[:, h % 4, 128:384], probs[:, h % 4, 128:384], srec[:, h, 1:2], None,
                                        ALU.mult)
                dve.drain().then_inc(probs_ready, 1)

            def layer_norm(n, l):
                for t in range(T):
                    for a in range(2):
                        s = slice(512 * a, 512 * a + 512)
                        nc.vector.scalar_tensor_tensor(X[:, t, s], X[:, t, s], ALPHA, quad[:, 2 * t + a, :],
                                                       ALU.mult, ALU.add)
                    dve.drain().then_inc(quad_free, 1)
                    for a in range(2):
                        nc.vector.bn_stats(bn[:, t, a, :], X[:, t, 512 * a:512 * a + 512])
                    dve.drain()
                    nc.vector.bn_aggr(mv[:, t, :], bn[:, t].rearrange("p a b -> p (a b)"))
                    dve.drain()
                    nc.vector.tensor_scalar(lv[:, t:t + 1], mv[:, t, 1:2], EPS, None,
                                            ALU.add).then_inc(ln_var, 1)
                dve.wait_ge(ln_full, l * 96 + 32 * (n + 1))
                for t in range(T):
                    dve.wait_ge(ln_rstd, l * (3 * T) + (n * T + t + 1))
                    nc.vector.scalar_tensor_tensor(X[:, t, :], X[:, t, :], mv[:, t, 0:1], ln_w[:, 0, :],
                                                   ALU.subtract, ALU.mult).then_inc(ln_read, 1)
                    dve.drain()
                    nc.vector.scalar_tensor_tensor(X[:, t, :], X[:, t, :], lr[:, t:t + 1], ln_w[:, 1, :],
                                                   ALU.mult, ALU.add).then_inc(ln_read, 1)
                    dve.drain().then_inc(x_ready, 1)

            dve.sem_inc(split_done, RAW_SLOTS)
            dve.wait_ge(start_full, 32)
            dve.sem_inc(x_ready, T)

            dve.wait_ge(pre_full, 16 * 6)
            a0, a1, a2, a3 = (ang[:, i, :] for i in range(4))
            nc.vector.tensor_copy(a0, pos_i.bitcast(I32))
            dve.drain()
            nc.vector.tensor_scalar(a0, a0, freq[:, 0:1], None, ALU.mult)
            dve.drain()
            nc.vector.tensor_scalar(a1, a0, 1.0 / TWO_PI, None, ALU.mult)
            dve.drain()
            nc.vector.tensor_scalar(a1, a1, ROUND_MAGIC, None, ALU.add)
            dve.drain()
            nc.vector.tensor_scalar(a1, a1, ROUND_MAGIC, None, ALU.subtract)
            dve.drain()
            for part in (TURN_HI, TURN_MID, TURN_LO):
                nc.vector.scalar_tensor_tensor(a0, a1, -part, a0, ALU.mult, ALU.add)
                dve.drain()
            nc.vector.tensor_scalar(a3, a0, PI_BELOW, -PI_BELOW, ALU.min, ALU.max)
            nc.vector.tensor_scalar(a1, a0, -1.0, None, ALU.mult)
            dve.drain()
            nc.vector.tensor_tensor(a2, a0, a1, ALU.max)
            dve.drain()
            nc.vector.tensor_scalar(a2, a2, -1.0, float(np.pi / 2), ALU.mult, ALU.add)
            dve.drain().then_inc(rope_arg, 1)
            dve.wait_ge(rope_sined, 1)
            nc.vector.tensor_scalar(rope_sin[:], rope_sin[:], freq[:, 1:2], None, ALU.mult)
            dve.wait_ge(rwhi, 1)
            nc.vector.tensor_tensor(rw_lo[:], rwraw, rw_hi[:].bitcast(F32), ALU.subtract)
            dve.drain()
            for j in range(PRO):
                dve.wait_ge(misc_ready, j + 1)
                t, c = j // 2, 4 * (j % 2)
                nc.vector.tensor_copy(memT[:, c:c + 4, t * P:(t + 1) * P],
                                      ring[:, j, :].rearrange("p (a b) -> p a b", a=4)).then_inc(dve_emptied, 1)
            dve.drain()

            NORMAL = 2048
            size = {1: DC * 160, U_OUT + 4: D, U_OUT + 5: D}

            with dve.Fori(0, DEPTH) as l:
                def split_pair(i):
                    dve.wait_ge(misc_ready, misc_done(f"pv{i}", l))
                    src = bank(f"pv{i}")[:, 0:SEQ]
                    nc.vector.tensor_copy(y_hi[:, 2 + i, :], src)
                    dve.drain()
                    nc.vector.tensor_tensor(y_lo[:, 2 + i, :], src, y_hi[:, 2 + i, :].bitcast(F32), ALU.subtract)
                    dve.drain().then_inc(dve_emptied, 1)
                    dve.drain().then_inc(y_ready, 1)

                def ahead(u):
                    lo(u + SPLIT_SLOTS, l, size.get(u + SPLIT_SLOTS, NORMAL))

                lo(0, l, NORMAL)
                lo_rotary(l)
                x_low("xa", l, 0)
                dve.wait_ge(small_full, l * SMALL_LAYER + SMALL_LAYER)
                for c in range(2):
                    src = wuq_in[:, c, :].rearrange("p (h n) -> p h n", h=MLA_HEADS)
                    rope = wuq[c][:, 512:768].rearrange("p (h n) -> p h n", h=MLA_HEADS)
                    swap = wuq[c][:, 768:1024].rearrange("p (h n) -> p h n", h=MLA_HEADS)
                    nc.vector.tensor_copy(wuq[c][:, 0:512].rearrange("p (h n) -> p h n", h=MLA_HEADS), src[:, :, 0:NOPE])
                    nc.vector.tensor_copy(rope, src[:, :, NOPE:])
                    nc.vector.tensor_copy(swap[:, :, 0:16], src[:, :, NOPE + 16:])
                    nc.vector.tensor_copy(swap[:, :, 16:32], src[:, :, NOPE:NOPE + 16])
                dve.drain().then_inc(wuq_ready, 1)
                nc.vector.memset(chp[:, :, 0:CONV_W - 1], 0.0)
                nc.vector.memset(pa[:, :, 0:PAD], 0.0)
                dve.wait_ge(act_emptied, emptied("cq", l))
                nc.vector.tensor_tensor(sq[:, 0:2, :], cT[:, 0:2, :], cT[:, 0:2, :], ALU.mult).then_inc(sq_ready, 1)
                ahead(0)
                dve.wait_ge(unit_used, used(1, l))
                kvb = bank("ckv")
                nc.vector.tensor_copy(cT[:, 2, :], kvb[:, 0:SEQ])
                nc.vector.tensor_tensor(kr[0:32], kvb[64:96, SEQ:], rope_cos[64:96], ALU.mult)
                nc.vector.tensor_tensor(rtmp[0:32, 0, :], kvb[96:128, SEQ:], rope_sin[96:128], ALU.mult)
                dve.drain().then_inc(dve_emptied, 1)
                nc.vector.tensor_tensor(sq[:, 2, :], cT[:, 2, :], cT[:, 2, :], ALU.mult).then_inc(sq_ready, 1)
                nc.vector.tensor_tensor(kr[0:32], kr[0:32], rtmp[0:32, 0, :], ALU.add)
                dve.drain()
                for g in range(1, 4):
                    nc.vector.tensor_copy(kr[32 * g:32 * g + 32], kr[0:32])
                dve.drain()
                nc.vector.memset(pb_[:, :, 0:1], 0.0)
                nc.vector.memset(pc[:, :, 0:2], 0.0)
                ahead(1)
                dve.wait_ge(act_emptied, emptied("v", l))
                gelu_poly(vz)
                dve.wait_ge(misc_ready, misc_done("ssq", l))
                nc.vector.tensor_scalar(ms[:, 0:2], bank("ssq")[:, 0:2], 1.0 / QL, EPS, ALU.mult,
                                        ALU.add).then_inc(dve_emptied, 1)
                dve.wait_ge(misc_ready, misc_done("ssk", l))
                nc.vector.tensor_scalar(ms[:, 2:4], bank("ssk")[:, 0:2], 1.0 / P, EPS, ALU.mult,
                                        ALU.add).then_inc(dve_emptied, 1)
                dve.drain().then_inc(ms_ready, 1)
                ahead(2)
                gelu_end(vz, 0, l)
                for t in range(T):
                    nc.vector.tensor_tensor_reduce(out=gt[:, t, :], in0=vz[:, t, :], in1=vz[:, t, :],
                                                   scale=0.25 / 256, scalar=EPS, op0=ALU.mult, op1=ALU.add,
                                                   accum_out=vms[:, t:t + 1])
                dve.drain().then_inc(vms_ready, 1)
                dve.wait_ge(act_emptied, emptied("u", l))
                gelu_poly(uz)
                dve.wait_ge(vrs_ready, l + 1)
                nc.vector.tensor_scalar(vrs[:], vrs[:], 0.5, None, ALU.mult)
                dve.drain()
                for t in range(T):
                    nc.vector.scalar_tensor_tensor(vz[:, t, :], vz[:, t, :], vrs[:, t:t + 1], vg[:], ALU.mult, ALU.mult)
                dve.drain().then_inc(v_ready, 1)
                dve.wait_ge(misc_ready, misc_done("rb0", l))
                for c in range(3):
                    nc.vector.scalar_tensor_tensor(cn[:, c, :], cT[:, c, :], qg[:, c:c + 1], bank2("rb0")[:, c // 2, :],
                                                   ALU.mult, ALU.mult)
                dve.drain().then_inc(dve_emptied, 1)
                ahead(3)
                gelu_end(uz, 1, l)
                ahead(4)
                cos2 = bass.AP(rope_cos[:].tensor, 0, [list(rope_cos[:].ap[0]), [0, 2], [1, SEQ]])
                sin2 = bass.AP(rope_sin[:].tensor, 0, [list(rope_sin[:].ap[0]), [0, 2], [1, SEQ]])
                dve.wait_ge(misc_ready, misc_done("qr", l))
                nc.vector.scalar_tensor_tensor(qr, bank2("qr"), MLA_SCALE, cos2, ALU.mult, ALU.mult).then_inc(dve_emptied, 1)
                dve.wait_ge(misc_ready, misc_done("qrs", l))
                nc.vector.scalar_tensor_tensor(rtmp, bank2("qrs"), MLA_SCALE, sin2, ALU.mult,
                                               ALU.mult).then_inc(dve_emptied, 1)
                dve.drain()
                nc.vector.tensor_tensor(qr, qr, rtmp, ALU.add)
                dve.drain().then_inc(rope_ready, 1)
                head_max(0, l)
                head_max(1, l)
                ahead(5)
                head_max(2, l)
                head_max(3, l)
                head_norm(0, l)
                head_norm(1, l)
                dve.wait_ge(act_emptied, emptied("h", l))
                nc.vector.tensor_tensor(chp[:, :, CONV_W - 1:], chp[:, :, CONV_W - 1:], zc, ALU.mult)
                dve.drain()
                ahead(6)
                for c in range(2):
                    nc.vector.tensor_scalar(zc[:, c, :], chp[:, c, 0:SEQ], cw[:, c, 0:1], None, ALU.mult)
                dve.drain()
                head_norm(2, l)
                head_norm(3, l)
                for k in range(1, CONV_W):
                    for c in range(2):
                        nc.vector.scalar_tensor_tensor(zc[:, c, :], chp[:, c, k:k + SEQ], cw[:, c, k:k + 1], zc[:, c, :],
                                                       ALU.mult, ALU.add)
                    dve.drain()
                nc.vector.tensor_tensor(zc, zc, zb, ALU.mult)
                dve.drain()
                split_y(6, 2, zc)
                head_max(4, l)
                head_max(5, l)
                ahead(7)
                dve.wait_ge(act_emptied, emptied("d", l))
                W = PAD + SEQ
                nc.vector.tensor_tensor(pb_[:, :, 1:], pa[:, :, 1:], pa[:, :, 0:W - 1], ALU.add)
                dve.drain()
                nc.vector.tensor_tensor(pc[:, :, 2:], pb_[:, :, 2:], pb_[:, :, 0:W - 2], ALU.add)
                dve.drain()
                nc.vector.tensor_tensor(pb_[:, 1, 4:], pc[:, 1, 4:], pc[:, 1, 0:W - 4], ALU.add)
                dve.drain()
                nc.vector.tensor_tensor(pc[64:, 1, 8:], pb_[64:, 1, 8:], pb_[64:, 1, 0:W - 8], ALU.add)
                dve.drain()
                halves = ((slice(0, 64), 0, pb_), (slice(64, P), 0, pc), (slice(0, 64), 1, pb_), (slice(64, P), 1, pc))
                for rows, c, s in halves:
                    nc.vector.tensor_tensor(s[rows, c, PAD:2 * PAD], s[rows, c, PAD:2 * PAD], pinv[rows, c, 1:], ALU.mult)
                dve.drain()
                for rows, c, s in halves:
                    nc.vector.scalar_tensor_tensor(gt[rows, c, :], s[rows, c, PAD:], pinv[rows, c, 0:1],
                                                   pa[rows, c, PAD:], ALU.mult, ALU.subtract)
                dve.drain().then_inc(pooled, 1)
                head_norm(4, l)
                head_norm(5, l)
                split_pair(0)
                dve.wait_ge(misc_ready, misc_done("mix", l))
                bs2 = bass.AP(bs[:].tensor, 0, [list(bs[:].ap[0]), [CHUNK, 2], [0, T], [1, CHUNK]])
                g4 = vz.rearrange("p a (t n) -> p a t n", t=T)
                nc.vector.tensor_tensor(g4, bank2("mix").rearrange("p a (t n) -> p a t n", t=T), bs2, ALU.add)
                dve.drain().then_inc(dve_emptied, 1)
                nc.vector.scalar_tensor_tensor(vz, vz, 0.5, uz, ALU.mult, ALU.mult)
                dve.drain()
                split_y(0, 2, vz)
                head_max(6, l)
                head_max(7, l)
                head_norm(6, l)
                head_norm(7, l)
                split_pair(1)
                dve.wait_ge(misc_ready, misc_done("yd", l))
                for c in range(2):
                    nc.vector.tensor_scalar(th[:, c, :], bank2("yd")[:, c, :], psc[:, c:c + 1], None, ALU.mult)
                dve.drain().then_inc(dve_emptied, 1)
                split_y(8, 2, th)
                ahead(8)
                split_pair(2)
                ahead(9)
                split_pair(3)
                for u in range(10, 14):
                    ahead(u)
                dve.wait_ge(memhl, l + 1)
                nc.vector.tensor_tensor(x_lo[:], memT[:], x_hi[:].bitcast(F32), ALU.subtract)
                dve.drain().then_inc(mem_split, 1)
                dve.wait_ge(unit_used, used(U_K - 1, l))
                layer_norm(0, l)
                for u in range(U_K, U_V + 4):
                    ahead(u)
                x_low("xb", l, 1)
                for i in range(4):
                    ahead(U_Q + i)
                for h in range(X_HEADS):
                    dve.wait_ge(misc_ready, misc_done(f"cs{h}", l))
                    nc.vector.tensor_reduce(smax[:, h, :], bank2(f"cs{h}"), AX_X, ALU.max, negate=True)
                    dve.drain().then_inc(xmax_ready, 1)
                for h in range(X_HEADS):
                    dve.wait_ge(act_emptied, emptied(f"cs{h}", l))
                    nc.vector.reciprocal(srec[:, h, :], ssum[:, h, :])
                    dve.drain()
                    for t in range(T):
                        nc.vector.tensor_scalar(xprobs[:, h, 256 * t:256 * t + 256], xprobs[:, h, 256 * t:256 * t + 256],
                                                srec[:, h, t:t + 1], None, ALU.mult)
                    dve.drain().then_inc(xprobs_ready, 1)
                for h in range(X_HEADS):
                    dve.wait_ge(act_emptied, emptied(f"cpv{h}", l))
                    split_y(2 * h, 2, qT[:, 2 * h:2 * h + 2, :])
                for i in range(2):
                    ahead(U_O + i)
                for k in range(3):
                    lo(U_MOE + k, l, NORMAL)
                dve.wait_ge(unit_used, used(U_O + 3, l))
                layer_norm(1, l)
                x_low("xc", l, 2)

                dve.wait_ge(misc_ready, misc_done("rt1", l))
                nc.vector.tensor_copy(rt[:, 0, 0], bank("rt0")[:, 0:E]).then_inc(dve_emptied, 1)
                nc.vector.tensor_copy(rt[:, 0, 1], bank("rt1")[:, 0:E]).then_inc(dve_emptied, 1)
                dve.drain().then_inc(logit, 1)
                dve.wait_ge(sig_exp, l + 1)
                score, sel, rank, cmp_, grp = rt[:, 1], rt[:, 2], rt[:, 3], rt[:, 4], rt[:, 5]
                nc.vector.tensor_scalar(score, score, 1.0, None, ALU.add)
                dve.drain()
                nc.vector.reciprocal(score, score)
                dve.drain()
                rbb = bass.AP(rb[:].tensor, 0, [list(rb[:].ap[0]), [0, T], [1, E]])
                nc.vector.tensor_tensor(sel, score, rbb, ALU.add)
                dve.drain()

                def g4v(v):
                    return v.rearrange("p t (g e) -> p (t g) e", e=PER_GROUP)

                def ranks(v, r, c):
                    nc.vector.memset(r, 0.0)
                    dve.drain()
                    n = v.shape[1]
                    for j in range(3):
                        for k in range(j + 1, 4):
                            nc.vector.tensor_tensor(c[:, :, 0:1], v[:, :, j:j + 1], v[:, :, k:k + 1], ALU.is_ge)
                            dve.drain()
                            nc.vector.tensor_tensor(r[:, :, k:k + 1], r[:, :, k:k + 1], c[:, :, 0:1], ALU.add)
                            nc.vector.scalar_tensor_tensor(r[:, :, j:j + 1], r[:, :, j:j + 1], 1.0, c[:, :, 0:1],
                                                           ALU.add, ALU.subtract)
                            dve.drain()

                s4, r4, c4 = g4v(sel), g4v(rank), g4v(cmp_)
                gs = grp[:, 0, 0:8].rearrange("p (a b) -> p a b", b=1)
                first = True
                for j in range(3):
                    for k in range(j + 1, 4):
                        dst = gs if first else c4[:, :, 0:1]
                        nc.vector.tensor_tensor(dst, s4[:, :, j:j + 1], s4[:, :, k:k + 1], ALU.add)
                        dve.drain()
                        if not first:
                            nc.vector.tensor_tensor(gs, gs, c4[:, :, 0:1], ALU.max)
                            dve.drain()
                        first = False
                ranks(s4, r4, c4)
                gsv = grp[:, 0, 0:8].rearrange("p (t g) -> p t g", t=T)
                grv = grp[:, 1, 0:8].rearrange("p (t g) -> p t g", t=T)
                gcv = rt[:, 6, 0, 0:8].rearrange("p (t g) -> p t g", t=T)
                ranks(gsv, grv, gcv)
                nc.vector.tensor_scalar(grv, grv, 1.0, None, ALU.is_lt)
                nc.vector.tensor_scalar(rank, rank, 2.0, None, ALU.is_lt)
                dve.drain().then_inc(member_ready, 1)
                nc.vector.tensor_tensor(rank, rank, score, ALU.mult)
                gg = grp[:, 1, 0:8]
                gb4 = bass.AP(gg.tensor, gg.offset, [list(gg.ap[0]), [1, 8], [0, PER_GROUP]])
                dve.drain()
                nc.vector.tensor_tensor(r4, r4, gb4, ALU.mult)
                dve.drain()
                nc.vector.tensor_reduce(grp[:, 0, 8:10], rank, AX_X, ALU.add)
                dve.drain()
                nc.vector.reciprocal(grp[:, 0, 10:12], grp[:, 0, 8:10])
                dve.drain()
                for t in range(T):
                    nc.vector.tensor_scalar(gates[:, t, :], rank[:, t, :], grp[:, 0, 10 + t:11 + t], None, ALU.mult)
                dve.drain().then_inc(gates_ready, 1)

                dve.wait_ge(placed, l + 1)
                counts = bank("rt0")[:, 256:256 + 3 * N_GROUPS]
                nc.vector.tensor_copy(place[:].rearrange("p t g -> p (t g)"), counts[:, 0:T * N_GROUPS])
                nc.vector.tensor_reduce(grp[:, 0, 12:13], counts[:, T * N_GROUPS:], AX_X, ALU.max)
                dve.drain()
                nc.vector.tensor_scalar(fits[:], grp[:, 0, 12:13], float(P), None, ALU.is_le)
                dve.drain().then_inc(fits_ready, 1)

                with dve.If(dve.value_load(fits[0:1, 0:1], min_val=0, max_val=1)):
                    for g in range(N_GROUPS):
                        for t in range(T):
                            nc.vector.tensor_scalar(to_slot(t)[:, g * P:(g + 1) * P], slots[:], place[:, t, g:g + 1],
                                                    grv[:, t, g:g + 1], ALU.is_equal, ALU.mult)
                    dve.drain().then_inc(slots_ready, 1)

                    def gather_low(pair):
                        for r in range(4):
                            dve.wait_ge(gath_hi, l * 8 + (4 * pair + r + 1))
                            nc.vector.tensor_tensor(x_lo[:, 2 * r:2 * r + 2, :],
                                                    ring[:, r % 2, :].rearrange("p (a b) -> p a b", a=2),
                                                    x_hi[:, 2 * r:2 * r + 2, :].bitcast(F32),
                                                    ALU.subtract).then_inc(gath_lo, 1)

                    def gated(k):
                        dve.wait_ge(moe_tanh, l * E + (k + 1))
                        nc.vector.scalar_tensor_tensor(s_t[:, k % 2, :], s_th[:, k % 2, :], 1.0, ring[:, 0, 0:FF],
                                                       ALU.add, ALU.mult).then_inc(dve_emptied, 1)

                    def times_up(k):
                        dve.drain()
                        dve.wait_ge(unit_used, used(up_unit(k), l))
                        nc.vector.scalar_tensor_tensor(s_t[:, k % 2, :], s_t[:, k % 2, :], slot_gates[:, k:k + 1],
                                                       ring[:, 1, 0:FF], ALU.mult, ALU.mult).then_inc(dve_emptied, 1)

                    def turned_low(k):
                        dve.wait_ge(turned_hi, l * E + (k + 1))
                        nc.vector.tensor_tensor(y_lo[:, k % 2, :], ring[:, 1, FF:2 * FF], y_hi[:, k % 2, :].bitcast(F32),
                                                ALU.subtract).then_inc(h_ready, 1)

                    def out_low(g):
                        dve.wait_ge(out_hi, l * N_GROUPS + (g + 1))
                        for a in range(2):
                            last = nc.vector.tensor_tensor(y_lo[:, 2 + 2 * a:4 + 2 * a, :],
                                                           ring[:, 2 + a, :].rearrange("p (a b) -> p a b", a=2),
                                                           y_hi[:, 2 + 2 * a:4 + 2 * a, :].bitcast(F32), ALU.subtract)
                        last.then_inc(out_split, 1)

                    gather_low(0)
                    dve.wait_ge(slot_gated, l + 1)
                    nc.vector.tensor_scalar(slot_gates[:], quad[:, 0, 0:E], 0.5, None, ALU.mult)
                    gated(0)
                    for k in range(1, E):
                        times_up(k - 1)
                        if k == E // 2:
                            gather_low(1)
                        lo(up_unit(k), l, NORMAL)
                        gated(k)
                        turned_low(k - 1)
                        lo(up_unit(k) + 1, l, NORMAL)
                        if k >= 5 and k % PER_GROUP == 1:
                            out_low(k // PER_GROUP - 1)
                        lo(up_unit(k) + 2, l, NORMAL)
                    times_up(E - 1)
                    turned_low(E - 1)
                    out_low(N_GROUPS - 1)
                with dve.Else():
                    def hidden(par, gates_of, u, i, e):
                        t = m_t[:, par, :]
                        dve.wait_ge(moe_tanh, l * E + (e + 1))
                        nc.vector.scalar_tensor_tensor(t, m_th, 1.0, ring[:, 2 * par, :], ALU.add,
                                                       ALU.mult).then_inc(dve_emptied, 1)
                        dve.drain()
                        dve.wait_ge(unit_used, used(u, l) + i)
                        nc.vector.tensor_tensor(t, t, ring[:, 2 * par + 1, :], ALU.mult).then_inc(dve_emptied, 1)
                        dve.drain()
                        t2 = t.rearrange("p (a b) -> p a b", a=2)
                        nc.vector.tensor_tensor(t2, t2, gates_of, ALU.mult)
                        dve.drain()
                        nc.vector.tensor_copy(y_hi[:, 2 * par:2 * par + 2, :], t2)
                        dve.drain()
                        nc.vector.tensor_tensor(y_lo[:, 2 * par:2 * par + 2, :], t2,
                                                y_hi[:, 2 * par:2 * par + 2, :].bitcast(F32),
                                                ALU.subtract).then_inc(h_ready, 1)
                        dve.drain()

                    def gate_rows(e):
                        a = gbc[:, 0, :]
                        return bass.AP(a.tensor, a.offset + e * SEQ, [list(a.ap[0]), [0, 2], [1, SEQ]])

                    def lo_step(k, i):
                        for u in range(up_unit(k), up_unit(k) + 3):
                            lo(u, l, NORMAL, i)

                    dve.wait_ge(act_emptied, emptied("gb7", l))
                    hidden(0, gate_rows(0), up_unit(0), 0, 0)
                    lo_step(1, 0)
                    hidden(1, gate_rows(1), up_unit(1), 0, 1)
                    lo_step(2, 0)
                    hidden(0, gate_rows(2), up_unit(2), 0, 2)
                    lo_step(3, 0)
                    with dve.Fori(1, STEPS) as i:
                        hidden(1, gate_rows(i * 2 + 1), up_unit(3) - 6, i * 6, i * 2 + 1)
                        lo_step(2, i)
                        hidden(0, gate_rows(i * 2 + 2), up_unit(2), i * 6, i * 2 + 2)
                        lo_step(3, i)
                    hidden(1, gate_rows(E - 1), up_unit(E - 1), 0, E - 1)
                    dve.sem_inc(slots_ready, 1)
                    dve.sem_inc(gath_lo, 8)
                    dve.sem_inc(out_split, N_GROUPS)
                dve.wait_ge(moe_done, l + 1)
                layer_norm(2, l)

        @block.tensor
        def _(pe):
            mm = nc.tensor.matmul

            def free(name, l):
                i = INDEX[name]
                if i >= 4:
                    before = JOBS[i - 4][0]
                    pe.wait_ge(act_emptied if JOBS[i - 4][1] == "act" else dve_emptied, emptied(before, l))
                else:
                    pe.wait_ge(dve_emptied, l * DVE_LAYER + PRO)
                return bank(name)

            def three(out, a_hi, a_lo, b_hi, b_lo, first, last):
                mm(out, a_hi, b_hi, start=first, stop=False)
                mm(out, a_hi, b_lo, start=False, stop=False)
                return mm(out, a_lo, b_hi, start=False, stop=last)

            def unit_views(u, k, n):
                return (unit_slot(u, 0, k * n).rearrange("p (k n) -> p k n", k=k),
                        unit_slot(u, 1, k * n).rearrange("p (k n) -> p k n", k=k))

            def rows_out(out, u, cols, l, n=256):
                h, lw = unit_views(u, DC, n)
                for k in range(DC):
                    r = three(out, cols(h[:, k, :]), cols(lw[:, k, :]), x_hi[:, k, :], x_lo[:, k, :], k == 0, k == DC - 1)
                return r

            def project(name, u, l, wait=True):
                pe.wait_ge(split_done, split(u, l))
                o = free(name, l)
                for c in range(2):
                    r = rows_out(o[:, c * SEQ:(c + 1) * SEQ], u, lambda v: v[:, c * P:(c + 1) * P], l)
                r.then_inc(unit_used, 1)

            def into_quad(a_hi, a_lo, c0, n, u, l, first, last, i=0):
                pe.wait_ge(split_done, split(u, l) + i)
                h, lw = unit_views(u, n, D)
                for k in range(n):
                    for t in range(T):
                        s = slice(t * P, (t + 1) * P)
                        for a in range(2):
                            r = three(quad[:, 2 * t + a, :], a_hi[:, c0 + k, s], a_lo[:, c0 + k, s],
                                      h[:, k, 512 * a:512 * a + 512], lw[:, k, 512 * a:512 * a + 512],
                                      first and k == 0, last and k == n - 1)
                r.then_inc(unit_used, 1)

            def transpose_x(name, l, n):
                for j in range(4):
                    t, c0 = j // 2, 4 * (j % 2)
                    pe.wait_ge(x_ready, l * (3 * T) + (n * T + t + 1))
                    o = free(f"{name}{j}", l)
                    for c in range(4):
                        src = X[:, t, :].rearrange("p (q c) -> p c q", c=DC)[:, c0 + c, :]
                        r = nc.tensor.transpose(o[:, c * P:(c + 1) * P], src, ident[:])
                    r.then_inc(misc_ready, 1)

            pe.sem_inc(unit_used, SPLIT_SLOTS)
            pe.wait_ge(ident_ready, 1)
            pe.wait_ge(start_full, 32)
            for j in range(PRO):
                t, c0 = j // 2, 4 * (j % 2)
                for c in range(4):
                    src = mem_in[:, t, :].rearrange("p (q c) -> p c q", c=DC)[:, c0 + c, :]
                    r = nc.tensor.transpose(ring[:, j, c * P:(c + 1) * P], src, ident[:])
                r.then_inc(misc_ready, 1)

            def scores(h, l):
                o = free(f"s{h}", l)
                n0, r0 = 64 * (h % 2), 32 * (h % 4)
                for t in range(T):
                    q, k = slice(t * P, (t + 1) * P), slice(0, (t + 1) * P)
                    d = o[:, 0:128] if t == 0 else o[:, 128:384]
                    mm(d, qn[n0:n0 + 64, h // 2, q], kn[n0:n0 + 64, h // 2, k], start=True, stop=False)
                    r = mm(d, qr[r0:r0 + 32, h // 4, q], kr[r0:r0 + 32, k], start=False, stop=True)
                r.then_inc(misc_ready, 1)

            def probs_t(h, l):
                pe.wait_ge(probs_ready, l * MLA_HEADS + (h + 1))
                o = free(f"pt{h}", l)
                for j, c in enumerate((0, 128, 256)):
                    r = nc.tensor.transpose(o[:, c:c + 128], probs[:, h % 4, c:c + 128], ident[:])
                r.then_inc(misc_ready, 1)

            def attend(i, l):
                o = free(f"pv{i}", l)
                pe.wait_ge(act_emptied, emptied(f"pt{2 * i + 1}", l))
                for h in (2 * i, 2 * i + 1):
                    rows = slice(64 * (h % 2), 64 * (h % 2) + 64)
                    mm(o[rows, 0:256], vv[:, 0, 64 * h:64 * h + 64], probsT[:, h % 2, 0:256], start=True, stop=False,
                       skip_group_check=True)
                    r = mm(o[rows, 128:256], vv[:, 1, 64 * h:64 * h + 64], probsT[:, h % 2, 256:384], start=False,
                           stop=True, skip_group_check=True)
                r.then_inc(misc_ready, 1)

            with pe.Fori(0, DEPTH) as l:
                transpose_x("xa", l, 0)
                pe.wait_ge(dve_emptied, emptied("xa3", l))
                project("cq", 0, l)
                pe.wait_ge(split_done, split(1, l))
                o = free("ckv", l)
                rows_out(o[:, 0:SEQ], 1, lambda v: v[:, 0:P], l, n=KV_COLS)
                rows_out(o[:, SEQ:], 1, lambda v: v[:, KV_COLS - P:], l, n=KV_COLS).then_inc(unit_used, 1)
                pe.wait_ge(split_done, split(2, l))
                o = free("v", l)
                h, lw = unit_views(2, DC, 256)
                for t in range(T):
                    s = slice(t * P, (t + 1) * P)
                    for k in range(DC):
                        r = three(o[:, t * 256:(t + 1) * 256], x_hi[:, k, s], x_lo[:, k, s], h[:, k, :], lw[:, k, :],
                                  k == 0, k == DC - 1)
                r.then_inc(unit_used, 1)
                for name, cs, n in (("ssq", (0, 1), 1), ("ssk", (2,), 2)):
                    pe.wait_ge(sq_ready, l * 2 + n)
                    o = free(name, l)
                    for t in range(T):
                        for c in cs:
                            r = mm(o[:, t:t + 1], sq[:, c, t * P:(t + 1) * P], ones[:, 0:1], start=c == cs[0],
                                   stop=c == cs[-1])
                    r.then_inc(misc_ready, 1)
                project("u", 3, l)
                pe.wait_ge(rs_ready, l + 1)
                o = free("rb0", l)
                for j in range(4):
                    r = mm(o[:, j * P:(j + 1) * P], rs[:, j:j + 1].to_broadcast([P, P]), ident[:], start=True, stop=True)
                r.then_inc(misc_ready, 1)
                project("b", 4, l)

                pe.wait_ge(dve_emptied, emptied("rb0", l))
                pe.wait_ge(small_full, l * SMALL_LAYER + SMALL_LAYER)

                def cols(v, off, dims):
                    return bass.AP(v.tensor, v.offset + off, [list(v.ap[0])] + dims)

                pe.wait_ge(wuq_ready, l + 1)
                for n, name in enumerate(("qn0", "qn1", "qr", "qrs")):
                    o = free(name, l)
                    for j in range(2):
                        for c in range(2):
                            r = mm(o[:, j * SEQ:(j + 1) * SEQ], wuq[c][:, (2 * n + j) * P:(2 * n + j + 1) * P],
                                   cn[:, c, :], start=c == 0, stop=c == 1)
                    r.then_inc(misc_ready, 1)
                HK = NOPE + MLA_V
                for i in range(2):
                    o = free(f"kn{i}", l)
                    for j in range(4):
                        h = 4 * i + j
                        r = mm(o[64 * (j % 2):64 * (j % 2) + 64, (j // 2) * SEQ:(j // 2 + 1) * SEQ],
                               wukv[:, h * HK:h * HK + NOPE], cn[:, 2, :], start=True, stop=True)
                    r.then_inc(misc_ready, 1)
                for t in range(T):
                    o = free(f"vv{t}", l)
                    mm(o, cn[:, 2, t * P:(t + 1) * P], cols(wukv[:], NOPE, [[HK, 8], [1, MLA_V]]), start=True,
                       stop=True).then_inc(misc_ready, 1)

                pe.wait_ge(act_emptied, emptied("vv1", l))
                pe.wait_ge(rope_ready, l + 1)
                scores(0, l)
                scores(1, l)
                project("c", 5, l)
                scores(2, l)
                scores(3, l)
                pe.wait_ge(ws_masked, l + 1)
                o = free("wst", l)
                for h in range(A_HEADS):
                    r = nc.tensor.transpose(o[:, h * CHUNK:(h + 1) * CHUNK], ws[:, h, :], ident[:])
                r.then_inc(misc_ready, 1)
                project("h", 6, l)
                probs_t(0, l)
                probs_t(1, l)
                scores(4, l)
                scores(5, l)
                project("d", 7, l)
                attend(0, l)
                pe.wait_ge(v_ready, l + 1)
                pe.wait_ge(act_emptied, emptied("wst", l))
                o = free("mix", l)
                for h in range(A_HEADS):
                    for t in range(T):
                        c = (h // 2) * SEQ + t * CHUNK
                        r = mm(o[64 * (h % 2):64 * (h % 2) + 64, c:c + CHUNK], vz[:, t, 64 * h:64 * h + 64], wsT[:, h, :],
                               start=True, stop=True)
                r.then_inc(misc_ready, 1)
                probs_t(2, l)
                probs_t(3, l)
                scores(6, l)
                scores(7, l)
                attend(1, l)
                probs_t(4, l)
                probs_t(5, l)
                pe.wait_ge(pooled, l + 1)
                o = free("yd", l)
                pe.sem_inc(pe_passed, 1)
                for g in range(4):
                    rows = slice(64 * (g % 2), 64 * (g % 2) + 64)
                    r = mm(o[rows, (g // 2) * SEQ:(g // 2 + 1) * SEQ], pw[rows, g // 2, :], gt[rows, g // 2, :],
                           start=True, stop=True)
                r.then_inc(misc_ready, 1)
                def out_unit(i, need):
                    c0, n = OUT_CHUNKS[i]
                    pe.wait_ge(y_ready, l * 11 + need)
                    into_quad(y_hi, y_lo, c0, n, U_OUT + i, l, i == 0, i == len(OUT_CHUNKS) - 1)

                out_unit(0, 1)
                attend(2, l)
                probs_t(6, l)
                probs_t(7, l)
                out_unit(1, 3)
                attend(3, l)
                out_unit(2, 5)
                out_unit(3, 5)
                out_unit(4, 6)
                out_unit(5, 7)
                pe.wait_ge(mem_split, l + 1)
                for i in range(4):
                    project(f"xk{i}", U_K + i, l)
                pe.wait_ge(quad_free, l * (3 * T) + T)
                for i in range(4):
                    into_quad(x_hi, x_lo, 2 * i, 2, U_V + i, l, i == 0, i == 3)
                transpose_x("xb", l, 1)
                pe.wait_ge(dve_emptied, emptied("xb3", l))
                for i in range(4):
                    project(f"xq{i}", U_Q + i, l)
                pe.wait_ge(quad_v, l + 1)
                for h in range(X_HEADS):
                    o = free(f"cs{h}", l)
                    pe.wait_ge(act_emptied, emptied(f"xq{h}", l))
                    for t in range(T):
                        for c in range(2):
                            r = mm(o[:, t * 256:(t + 1) * 256], qT[:, 2 * h + c, t * P:(t + 1) * P], kT[:, 2 * h + c, :],
                                   start=c == 0, stop=c == 1)
                    r.then_inc(misc_ready, 1)
                for h in range(X_HEADS):
                    pe.wait_ge(xprobs_ready, l * X_HEADS + (h + 1))
                    o = free(f"cpt{h}", l)
                    for m in range(2):
                        for t in range(T):
                            c = 256 * m + 128 * t
                            r = nc.tensor.transpose(o[:, c:c + P], xprobs[:, h, 256 * t + 128 * m:256 * t + 128 * m + P],
                                                    ident[:])
                    r.then_inc(misc_ready, 1)
                    o = free(f"cpv{h}", l)
                    pe.wait_ge(act_emptied, emptied(f"cpt{h}", l))
                    for c in range(2):
                        for m in range(2):
                            r = mm(o[:, c * SEQ:(c + 1) * SEQ], xv[:, m, 256 * h + 128 * c:256 * h + 128 * c + P],
                                   xprobsT[:, h % 2, 256 * m:256 * m + 256], start=m == 0, stop=m == 1)
                    r.then_inc(misc_ready, 1)
                for i in range(4):
                    pe.wait_ge(y_ready, l * 11 + (8 + i))
                    into_quad(y_hi, y_lo, 2 * i, 2, U_O + i, l, i == 0, i == 3)
                transpose_x("xc", l, 2)
                pe.wait_ge(dve_emptied, emptied("xc3", l))
                for t in range(T):
                    o = free(f"rt{t}", l)
                    s = slice(t * P, (t + 1) * P)
                    for k in range(DC):
                        r = three(o[:, 0:E], x_hi[:, k, s], x_lo[:, k, s], rw_hi[:, k, :], rw_lo[:, k, :],
                                  k == 0, k == DC - 1)
                    r.then_inc(misc_ready, 1)
                pe.wait_ge(member_ready, l + 1)
                counts = bank("rt0")[:, 256:256 + 3 * N_GROUPS]
                every = ones[:, 0:1].to_broadcast([P, P])
                member = [rt[:, 5, 1, 0:8].rearrange("p (t g) -> p t g", t=T)[:, t, :] for t in range(T)]
                mm(counts[:, 0:4], before[:], member[0], start=True, stop=True)
                mm(counts[:, 4:8], every, member[0], start=True, stop=False)
                mm(counts[:, 4:8], before[:], member[1], start=False, stop=True)
                mm(counts[:, 8:12], every, member[0], start=True, stop=False)
                mm(counts[:, 8:12], every, member[1], start=False, stop=True).then_inc(placed, 1)

                pe.wait_ge(fits_ready, l + 1)
                pe.sem_inc(pe_passed, 1)
                with pe.If(pe.value_load(fits[0:1, 0:1], min_val=0, max_val=1)):
                    pe.sem_inc(misc_ready, 8)

                    def gather(pair):
                        for r in range(4):
                            if r < 2 and pair:
                                pe.wait_ge(dve_emptied, l * DVE_LAYER + (DVE_AHEAD + E - 1 + r))
                            elif r >= 2:
                                pe.wait_ge(gath_lo, l * 8 + (4 * pair + r - 1))
                            for c in range(2):
                                o = ring[:, r % 2, c * 2 * P:(c + 1) * 2 * P]
                                for t in range(T):
                                    sl = (y_hi, y_lo)[t][:, 8 + pair, :]
                                    mm(o, xn_hi[:, t, 2 * r + c, :], sl, start=t == 0, stop=False)
                                    last = mm(o, xn_lo[:, t, 2 * r + c, :], sl, start=False, stop=t == T - 1)
                            last.then_inc(gathered, 1)

                    def project_slots(b, u, g):
                        pe.wait_ge(split_done, split(u, l))
                        h, lw = unit_views(u, DC, FF)
                        s = slice(P * (g % 2), P * (g % 2) + P)
                        for c in range(DC):
                            r = three(ring[:, b, 0:FF], x_hi[:, c, s], x_lo[:, c, s], h[:, c, :], lw[:, c, :],
                                      c == 0, c == DC - 1)
                        r.then_inc(unit_used, 1)

                    def turn(k):
                        pe.wait_ge(dve_emptied, l * DVE_LAYER + (DVE_AHEAD + 2 * (k + 1)))
                        for c in range(2):
                            r = nc.tensor.transpose(ring[:, 1, FF + c * P:FF + (c + 1) * P],
                                                    s_t[:, k % 2, c * P:(c + 1) * P], ident[:])
                        r.then_inc(turned, 1)

                    def down(k):
                        pe.wait_ge(split_done, split(down_unit(k), l))
                        pe.wait_ge(h_ready, l * E + (k + 1))
                        if k % PER_GROUP == 0 and k:
                            pe.wait_ge(out_split, l * N_GROUPS + k // PER_GROUP)
                        h, lw = unit_views(down_unit(k), 2, D)
                        for c in range(2):
                            s = slice(c * P, (c + 1) * P)
                            for a in range(2):
                                r = three(ring[:, 2 + a, :], y_hi[:, k % 2, s], y_lo[:, k % 2, s],
                                          h[:, c, 512 * a:512 * a + 512], lw[:, c, 512 * a:512 * a + 512],
                                          k % PER_GROUP == 0 and c == 0, k % PER_GROUP == PER_GROUP - 1 and c == 1)
                        r.then_inc(unit_used, 1)

                    def scatter(g):
                        pe.wait_ge(out_split, l * N_GROUPS + (g + 1))
                        for t in range(T):
                            for a in range(2):
                                for i, y in enumerate((y_hi, y_lo)):
                                    r = mm(quad[:, 2 * t + a, :], to_token[:, g, t * P:(t + 1) * P],
                                           y[:, 2 + 2 * a:4 + 2 * a, :].rearrange("p a b -> p (a b)"),
                                           start=g == 0 and i == 0, stop=g == N_GROUPS - 1 and i == 1)
                        return r

                    pe.wait_ge(slots_ready, l + 1)
                    pe.wait_ge(xn_lo_done, l + 1)
                    gather(0)
                    pe.wait_ge(gates_ready, l + 1)
                    pe.wait_ge(quad_free, l * (3 * T) + 2 * T)
                    for g in range(N_GROUPS):
                        for t in range(T):
                            r = mm(quad[:, 0, 4 * g:4 * g + 4], to_slot(t)[:, g * P:(g + 1) * P].bitcast(F32),
                                   gates[:, t, 4 * g:4 * g + 4], start=t == 0, stop=t == T - 1)
                    r.then_inc(slot_gated, 1)
                    for g in range(N_GROUPS):
                        for t in range(T):
                            c = (g % 2) * SEQ + t * P
                            r = nc.tensor.transpose(ring[:, 2 + g // 2, c:c + P],
                                                    to_slot(t)[:, g * P:(g + 1) * P].bitcast(F32), ident[:])
                    r.then_inc(to_token_done, 1)
                    pe.wait_ge(gath_lo, l * 8 + 4)
                    for k in range(E):
                        if k == E // 2:
                            gather(1)
                            pe.wait_ge(gath_lo, l * 8 + 8)
                        elif k:
                            pe.wait_ge(dve_emptied, l * DVE_LAYER + (DVE_AHEAD + 2 * k - 1))
                        project_slots(0, gate_unit(k), k // PER_GROUP)
                        if k:
                            turn(k - 1)
                        if k == 2:
                            pe.wait_ge(to_token_moved, l + 1)
                        if k >= 6 and k % PER_GROUP == 2:
                            scatter(k // PER_GROUP - 1)
                        if k >= 2:
                            down(k - 2)
                        if k:
                            pe.wait_ge(h_ready, l * E + k)
                        project_slots(1, up_unit(k), k // PER_GROUP)
                    down(E - 2)
                    turn(E - 1)
                    down(E - 1)
                    scatter(N_GROUPS - 1).then_inc(moe_done, 1)
                with pe.Else():
                    pe.wait_ge(gates_ready, l + 1)
                    for i in range(8):
                        o = free(f"gb{i}", l)
                        for j in range(2):
                            for t in range(T):
                                r = mm(o[:, j * SEQ + t * P:j * SEQ + (t + 1) * P],
                                       gates[:, t, 2 * i + j:2 * i + j + 1].to_broadcast([P, P]), ident[:],
                                       start=True, stop=True)
                        r.then_inc(misc_ready, 1)

                    def moe_in(b, u, i):
                        pe.wait_ge(split_done, split(u, l) + i)
                        for c in range(2):
                            r = rows_out(ring[:, b, c * SEQ:(c + 1) * SEQ], u, lambda v: v[:, c * P:(c + 1) * P], l)
                        r.then_inc(unit_used, 1)

                    def moe_down(par, u, i, e, first=False, last=False):
                        pe.wait_ge(h_ready, l * E + (e + 1))
                        into_quad(y_hi, y_lo, 2 * par, 2, u, l, first, last, i)

                    pe.wait_ge(act_emptied, emptied("gb7", l))
                    for k in range(2):
                        moe_in(2 * k, gate_unit(k), 0)
                        moe_in(2 * k + 1, up_unit(k), 0)
                    pe.wait_ge(quad_free, l * (3 * T) + 2 * T)

                    def step(k, i, e, first=False):
                        pe.wait_ge(dve_emptied, l * DVE_LAYER + e * 2 + (DVE_AHEAD + 2 * k - 2))
                        moe_in(2 * (k % 2), gate_unit(k), i)
                        moe_down(k % 2, down_unit(k - 2), i, e + (k - 2), first=first)
                        moe_in(2 * (k % 2) + 1, up_unit(k), i)

                    step(2, 0, 0, first=True)
                    step(3, 0, 0)
                    with pe.Fori(1, STEPS) as i:
                        step(2, i * 6, i * 2)
                        step(3, i * 6, i * 2)
                    moe_down(0, down_unit(E - 2), 0, E - 2)
                    moe_down(1, down_unit(E - 1), 0, E - 1, last=True)
                    pe.sem_inc(gathered, 8)
                    pe.sem_inc(slot_gated, 1)
                    pe.sem_inc(to_token_done, 1)
                    pe.sem_inc(turned, E)
                    pe.drain().then_inc(moe_done, 1)


_INS = ['x', 'mem', 'positions', 'w_in', 'gmlp_v_norm_g', 'gmlp_w_s', 'gmlp_b_s', 'mla_q_norm_g', 'mla_w_uq',
        'mla_kv_norm_g', 'mla_w_ukv', 'conv_w', 'pool_w', 'pool_scale', 'w_out', 'ln1_g', 'ln1_b', 'xattn_wq',
        'xattn_wk', 'xattn_wv', 'xattn_wo', 'ln2_g', 'ln2_b', 'router_w', 'router_b', 'moe_w_gate', 'moe_w_up',
        'moe_w_down', 'ln3_g', 'ln3_b']


def shape_constants():
    half = ROPE // 2
    row = np.arange(P)
    freq = (ROPE_BASE ** (-(2.0 * (row % half)) / ROPE)).astype(np.float32)
    sign = np.where(row % ROPE < half, -1.0, 1.0).astype(np.float32)
    inv = np.zeros((P, 2, PAD + 1), np.float32)
    for g, w in enumerate(POOL_WINDOWS):
        rows = slice(64 * (g % 2), 64 * (g % 2) + 64)
        inv[rows, g // 2, 0] = 1.0 / w
        inv[rows, g // 2, 1:] = w / np.minimum(np.arange(1, PAD + 1), w)
    return {"rope_freq": freq, "rope_sign": sign, "pool_inv": inv}


def kernel(**inputs):
    import concourse.bacc as _bacc
    from concourse.bass_utils import run_bass_kernel_spmd as _run

    nc = _bacc.Bacc("TRN2", target_bir_lowering=False, num_devices=1)
    arrays, args = {}, []
    given = {name: np.ascontiguousarray(inputs[name]) for name in _INS}
    for name, a in {**given, **shape_constants()}.items():
        arrays[f"in_{name}"] = a
        args.append(nc.dram_tensor(f"in_{name}", a.shape, mybir.dt.from_np(a.dtype), kind="ExternalInput").ap())
    shape = inputs["x"].shape
    args.append(nc.dram_tensor("out_x", list(shape), F32, kind="ExternalOutput").ap())
    hybrid_trunk_kernel(nc, *args)
    r = _run(nc, [arrays], core_ids=[0])
    return r.results[0]["out_x"]
```

```python
from contextlib import ExitStack

import numpy as np

import concourse.bass as bass
from concourse import mybir

F32 = mybir.dt.float32
F32R = mybir.dt.float32r
BF16 = mybir.dt.bfloat16
I32 = mybir.dt.int32
ALU = mybir.AluOpType
ACT = mybir.ActivationFunctionType
AX_X = mybir.AxisListType.X

P = 128
CHUNK = 128
A_HEADS, A_DIM = 4, 64
MLA_HEADS, NOPE, ROPE, MLA_V = 8, 64, 32, 64
ROPE_BASE = 10000.0
POOL_WINDOWS = (2, 4, 8, 16)
PAD = max(POOL_WINDOWS)
CONV_W = 3
X_HEADS = 4
N_GROUPS, PER_GROUP = 4, 4
EPS = 1e-6
MLA_SCALE = float(NOPE + ROPE) ** -0.5
GELU_CUBIC = 0.044715
GELU_SCALE = float(np.sqrt(2.0 / np.pi))
MASKED = -1e30
TWO_PI = 2.0 * np.pi
TURN_HI = float(np.float32(6.28125))
TURN_MID = float(np.float32(np.round((TWO_PI - 6.28125) * 2.0**21) / 2.0**21))
TURN_LO = float(np.float32(TWO_PI - TURN_HI - TURN_MID))
ROUND_MAGIC = 1.5 * 2.0**23
PI_BELOW = 3.1415925

RAW_SLOTS = 6
SPLIT_SLOTS = 2

IN_UNITS = ["cq", "ckv", "v", "u", "b", "c", "h", "d"]
U_K = len(IN_UNITS)
K_EARLY = 3
U_OUT = U_K + K_EARLY
OUT_CHUNKS = [(6, 2), (0, 2), (8, 2), (2, 2), (4, 1), (5, 1)]
U_K_LATE = U_OUT + len(OUT_CHUNKS)
K_UNITS = [U_K, U_K + 1, U_K + 2, U_K_LATE]
U_V = U_K_LATE + 1
U_Q = U_V + 4
U_O = U_Q + 4
U_MOE = U_O + 4


def ring_jobs():
    jobs = [(f"xa{i}", "dve") for i in range(4)]
    jobs += [("cq", "act"), ("ckv", "dve"), ("v", "act"), ("ssq", "dve"), ("ssk", "dve"), ("u", "act"),
             ("rb0", "dve"), ("b", "act")]
    jobs += [("qn0", "act"), ("qn1", "act"), ("qr", "dve"), ("qrs", "dve"), ("kn0", "act"), ("kn1", "act"),
             ("vv0", "act"), ("vv1", "act")]
    jobs += [("s0", "act"), ("s1", "act"), ("c", "act"), ("s2", "act"), ("s3", "act"), ("wst", "act"), ("h", "act"),
             ("pt0", "act"), ("pt1", "act"), ("s4", "act"), ("s5", "act"), ("d", "act")]
    jobs += [(f"mt{i}", "dve") for i in range(4)]
    jobs += [("pv0", "dve"), ("xk0", "act"), ("mix", "dve"), ("pt2", "act"), ("pt3", "act"), ("s6", "act"),
             ("s7", "act"), ("xk1", "act"), ("pv1", "dve"), ("pt4", "act"), ("pt5", "act"), ("xk2", "act"),
             ("yd", "dve"), ("pv2", "dve"), ("pt6", "act"), ("pt7", "act"), ("pv3", "dve"), ("xk3", "act")]
    jobs += [(f"xb{i}", "dve") for i in range(4)]
    jobs += [(f"xq{i}", "act") for i in range(4)]
    jobs += [(f"cs{i}", "act") for i in range(4)]
    jobs += [("cpt0", "act")]
    for i in range(4):
        jobs += ([(f"cpt{i + 1}", "act")] if i < 3 else []) + [(f"cpv{i}", "act")]
    jobs += [(f"xc{i}", "dve") for i in range(4)]
    jobs += [("rt0", "act"), ("rt1", "act")]
    jobs += [(f"gb{i}", "act") for i in range(8)]
    return jobs


def hybrid_trunk_kernel(nc, x, mem, positions, w_in, gmlp_v_norm_g, gmlp_w_s, gmlp_b_s, mla_q_norm_g,
                        mla_w_uq, mla_kv_norm_g, mla_w_ukv, conv_w, pool_w, pool_scale, w_out, ln1_g,
                        ln1_b, xattn_wq, xattn_wk, xattn_wv, xattn_wo, ln2_g, ln2_b, router_w, router_b,
                        moe_w_gate, moe_w_up, moe_w_down, ln3_g, ln3_b, rope_freq, rope_sign, pool_inv, pair_order, out):
    _, SEQ, D = x.shape
    DEPTH = w_in.shape[0]
    E = router_w.shape[1]
    T = SEQ // P
    DC = D // P
    MIX = w_out.shape[1]
    YC = MIX // P
    FF = moe_w_gate.shape[3]
    QL = mla_w_uq.shape[1]
    ALPHA = float((2 * DEPTH) ** 0.25)
    assert T == 2 and DC == 8 and YC == 10 and FF == 256 and E == 16 and QL == 256

    UNITS = U_MOE + 3 * E
    JOBS = ring_jobs()
    assert len(JOBS) % 4 == 0, "the banks must come round with the layer"
    INDEX = {name: i for i, (name, _) in enumerate(JOBS)}
    unit_jobs = set(IN_UNITS) | {f"xk{i}" for i in range(4)} | {f"xq{i}" for i in range(4)}
    ACT_LAYER = sum(by == "act" for _, by in JOBS)
    DVE_LAYER = sum(by == "dve" for _, by in JOBS) + 2 * E
    MISC_LAYER = sum(n not in unit_jobs for n, _ in JOBS)
    PRO = 1

    def emptied(name, l):
        i = INDEX[name]
        by = JOBS[i][1]
        n = sum(b == by for _, b in JOBS[:i + 1])
        return (l * ACT_LAYER + n) if by == "act" else (l * DVE_LAYER + n + PRO)

    def misc_done(name, l):
        return l * MISC_LAYER + sum(n not in unit_jobs for n, _ in JOBS[:INDEX[name] + 1]) + PRO

    def used(u, l):
        return l * UNITS + (u + 1 + SPLIT_SLOTS)

    def split(u, l):
        return l * UNITS + (u + 1 + RAW_SLOTS)

    with ExitStack() as ctx:
        def sb(name, shape, dt=F32):
            return ctx.enter_context(nc.sbuf_tensor(name, shape, dt))

        def sem(name):
            return ctx.enter_context(nc.semaphore(name))

        raw = sb("raw", [P, RAW_SLOTS, 2048])
        w_hi = sb("w_hi", [P, SPLIT_SLOTS, 2048], F32R)
        w_lo = sb("w_lo", [P, SPLIT_SLOTS, 2048], F32R)
        X = sb("X", [P, T, D])
        x_hi = sb("x_hi", [P, DC, SEQ], F32R)
        x_lo = sb("x_lo", [P, DC, SEQ], F32R)
        mem_kT = sb("mem_kT", [P, T * D])
        y_hi = sb("y_hi", [P, YC, SEQ], F32R)
        y_lo = sb("y_lo", [P, YC, SEQ], F32R)
        ln_w = sb("ln_w", [P, 2, D])
        wukv = sb("wukv", [P, MLA_HEADS * (NOPE + MLA_V)])
        ws = sb("ws", [P, A_HEADS, CHUNK])
        wsT = sb("wsT", [P, A_HEADS, CHUNK])
        bs = sb("bs", [P, 2, CHUNK])
        vg = sb("vg", [P, 256])
        pw = sb("pw", [P, 2, 64])
        cw = sb("cw", [P, 2, CONV_W])
        psc = sb("psc", [P, 2])
        qg = sb("qg", [P, 3])
        rope_cos = sb("rope_cos", [P, SEQ])
        rope_sin = sb("rope_sin", [P, SEQ])
        freq = sb("freq", [P, 2])
        ident = sb("ident", [P, P])
        causal = sb("causal", [P, P])
        ones = sb("ones", [P, 2])
        minus_half = sb("minus_half", [P, 4])
        order = sb("order", [P, PER_GROUP, PER_GROUP])
        pinv = sb("pinv", [P, 2, PAD + 1])
        rw = sb("rw", [P, 3 * P], F32R)
        rw_hi, rw_lo = (rw[:, i * P:(i + 1) * P].rearrange("p (c e) -> p c e", c=DC) for i in range(2))
        rb = sb("rb", [P, E])
        ms = sb("ms", [P, 4])
        rs = sb("rs", [P, 4])
        vms = sb("vms", [P, 2])
        vrs = sb("vrs", [P, 2])
        smax = sb("smax", [P, 8, 2])
        ssum = sb("ssum", [P, 8, 2])
        srec = sb("srec", [P, 8, 2])
        bn = sb("bn", [P, T, 2, 6])
        mv = sb("mv", [P, T, 2])
        lv = sb("lv", [P, T])
        lr = sb("lr", [P, T])
        minus_mean = sb("minus_mean", [P, 1])
        about_mean = sb("about_mean", [P, 1])
        gates = sb("gates", [P, T, E])
        before = sb("before", [P, P])
        slots = sb("slots", [P, P], BF16)
        place = sb("place", [P, T, N_GROUPS])
        slot_gates = sb("slot_gates", [P, E])
        fits = sb("fits", [P, 1], I32)
        ARENA = -(-nc.sbuf_base // 32) * 32
        arena = sb("arena", [P, 11632])

        def rounded(name, off, *shape):
            return nc.alloc_sbuf_tensor_at(name, [P, *shape], F32R, offset=ARENA + 4 * off)

        def at(off, *shape):
            n = int(np.prod(shape))
            v = arena[:, off:off + n]
            if len(shape) == 2:
                v = v.rearrange("p (a b) -> p a b", a=shape[0])
            return v

        cT = at(0, 4, SEQ)
        sq = at(1024, 3, SEQ)
        cn = at(1792, 3, SEQ)
        probs = at(1024, 4, 384)
        probsT = at(0, 2, 384)
        qn = at(2560, 4, SEQ)
        qr = at(3584, 2, SEQ)
        kn = at(4096, 4, SEQ)
        kr = at(5120, SEQ)
        vv = at(5376, T, 512)
        vz = at(6400, T, 256)
        gt = at(6912, 2, 256)
        th = at(7424, 2, 256)
        uz = at(7936, 2, 256)
        zb = at(8448, 2, 256)
        zc = at(8960, 2, 256)
        rtmp = zc
        chp = at(9472, 2, CONV_W - 1 + SEQ)
        pa = at(10000, 2, PAD + SEQ)
        pb_ = at(10544, 2, PAD + SEQ)
        pc = at(11088, 2, PAD + SEQ)
        wuq_in = at(10096, 2, MLA_HEADS * (NOPE + ROPE))
        wuq = [at(4096 + 1280 * c, 1024) for c in range(2)]
        passed = at(0, D)
        mem_in = mem_kT[:].rearrange("p (t d) -> p t d", t=T)
        kT = mem_kT[:].rearrange("p (c n) -> p c n", c=DC)
        xv = at(2048, T, D)
        qT = at(4096, DC, SEQ)
        xprobs = at(6144, 4, 512)
        xprobsT = at(8192, 2, 512)
        gbc = at(0, E, SEQ)
        m_th = at(4096, 512)
        m_t = at(4608, 2, 512)
        rt = at(5632, 7, T * E).rearrange("p a (t e) -> p a t e", t=T)
        logitsT = at(4096, SEQ)
        precede = at(4352, 8, PER_GROUP * PER_GROUP)
        precede2 = at(4480, 8, PER_GROUP * PER_GROUP)
        w_third = [rounded("w_third_hi", 6000, 2048), rounded("w_third_lo", 8048, 2048)]
        xn_hi = rounded("xn_hi", 0, T, DC, P)
        xn_lo = rounded("xn_lo", 2048, T, DC, P)
        s_t = at(4096, 2, FF)
        s_th = wsT[:].rearrange("p a b -> p (a b)").rearrange("p (a b) -> p a b", a=2)
        to_token = rounded("to_token", 4608, N_GROUPS, SEQ)
        ang = at(2048, 4, SEQ)
        pos_i = at(3072, SEQ)
        rwraw = at(3328, DC, E)

        ring = ctx.enter_context(nc.psum_tensor("ring", [P, 4, 512], F32))
        quad = ctx.enter_context(nc.psum_tensor("quad", [P, 4, 512], F32))

        def bank(name):
            return ring[:, INDEX[name] % 4, :]

        def to_slot(t):
            return (y_hi, y_lo)[t][:, 8:10, :].rearrange("p a b -> p (a b)")

        def gather_bank(pair, r):
            return ring[:, r % (2 if pair else 4), :]

        def bank2(name):
            return bank(name).rearrange("p (a b) -> p a b", a=2)

        raw_full = [sem(f"raw_full{i}") for i in range(RAW_SLOTS)]
        hi_done = sem("hi_done")
        split_done = sem("split_done")
        unit_used = sem("unit_used")
        misc_ready = sem("misc_ready")
        act_emptied = sem("act_emptied")
        dve_emptied = sem("dve_emptied")
        quad_free = sem("quad_free")
        values_moved = sem("values_moved")
        ident_ready = sem("ident_ready")
        sp_passed = sem("sp_passed")
        pe_passed = sem("pe_passed")
        act_passed = sem("act_passed")
        xhi_done = sem("xhi_done")
        start_full = sem("start_full")
        pre_full = sem("pre_full")
        rw_full = sem("rw_full")
        const_full = sem("const_full")
        small_full = sem("small_full")
        ln_full = sem("ln_full")
        ln_read = sem("ln_read")
        ln_var = sem("ln_var")
        ln_rstd = sem("ln_rstd")
        ln_sum = sem("ln_sum")
        ln_stats = sem("ln_stats")
        x_ready = sem("x_ready")
        ws_masked = sem("ws_masked")
        sq_ready = sem("sq_ready")
        wuq_ready = sem("wuq_ready")
        ms_ready = sem("ms_ready")
        rs_ready = sem("rs_ready")
        vms_ready = sem("vms_ready")
        vrs_ready = sem("vrs_ready")
        gelu_arg = sem("gelu_arg")
        gelu_tanh = sem("gelu_tanh")
        v_ready = sem("v_ready")
        rope_ready = sem("rope_ready")
        max_ready = sem("max_ready")
        probs_ready = sem("probs_ready")
        pooled = sem("pooled")
        y_ready = sem("y_ready")
        mem_full = sem("mem_full")
        quad_ready = sem("quad_ready")
        xmax_ready = sem("xmax_ready")
        xprobs_ready = sem("xprobs_ready")
        gates_ready = sem("gates_ready")
        xn_hi_done = sem("xn_hi_done")
        xn_lo_done = sem("xn_lo_done")
        member_ready = sem("member_ready")
        placed = sem("placed")
        fits_ready = sem("fits_ready")
        slots_ready = sem("slots_ready")
        gathered = sem("gathered")
        gath_hi = sem("gath_hi")
        gath_lo = sem("gath_lo")
        slot_gated = sem("slot_gated")
        to_token_done = sem("to_token_done")
        to_token_moved = sem("to_token_moved")
        turned = sem("turned")
        turned_hi = sem("turned_hi")
        half_out = sem("half_out")
        out_hi = sem("out_hi")
        out_split = sem("out_split")
        moe_done = sem("moe_done")
        moe_tanh = sem("moe_tanh")
        h_ready = sem("h_ready")
        rope_arg = sem("rope_arg")
        rope_sined = sem("rope_sined")
        rwhi = sem("rwhi")
        stored = sem("stored")

        block = ctx.enter_context(nc.Block())

        STEPS = (E - 2) // 2

        def gate_unit(k):
            return U_MOE + (2 * k if k < 2 else 3 * k - 2)

        def up_unit(k):
            return U_MOE + (1 if k == 0 else 3 * k)

        def down_unit(k):
            return U_MOE + 3 * k + 5 if k < E - 2 else UNITS - E + k

        def slot(u):
            return u % SPLIT_SLOTS if u < U_MOE else (u - U_MOE + 2) % 3

        def slot_before(u):
            return u - (SPLIT_SLOTS if u < U_MOE else 3)

        def unit_slot(u, part, n):
            k = slot(u)
            return (w_third[part][:, 0:n] if k == 2 else (w_hi, w_lo)[part][:, k, 0:n])

        KV_COLS = 192
        KV_PIECES = ((slice(0, 160), slice(0, 160)), (slice(160, 176), slice(144, 160)), (slice(176, 192), slice(128, 144)))

        def kv_views(dst):
            return (dst[:, 1 % SPLIT_SLOTS, 0:DC * KV_COLS].rearrange("p (k n) -> p k n", k=DC),
                    raw[:, 1 % RAW_SLOTS, 0:DC * 160].rearrange("p (k n) -> p k n", k=DC))

        @block.sync
        def _(sp):
            def load(u, l, src, shape, i=0):
                sp.wait_ge(split_done, split(u, l) - RAW_SLOTS + i)
                sp.sem_inc(sp_passed, 1)
                n = int(np.prod(shape))
                dst = raw[:, u % RAW_SLOTS, 0:n].rearrange("p (a b) -> p a b", a=shape[0])
                sp.dma_start(dst, src).then_inc(raw_full[u % RAW_SLOTS], 16)

            def by_columns(w, c0, n):
                return w[:, c0:c0 + n].rearrange("(p c) n -> p c n", c=DC)

            def expert(l, e, what, u, i):
                if what == "d":
                    load(u, l, moe_w_down[l, e].rearrange("(c p) n -> p c n", p=P), (2, D), i)
                else:
                    w = moe_w_gate if what == "g" else moe_w_up
                    load(u, l, w[l, e].rearrange("(p c) n -> p c n", c=DC), (DC, FF), i)

            with nc.allow_non_contiguous_dma(reason="small vectors, one element a partition"):
                sp.dma_start(pos_i.bitcast(I32), positions[0].partition_broadcast(P)).then_inc(pre_full, 16)
                sp.dma_start(freq[:, 0:1], rope_freq.rearrange("(p a) -> p a", a=1)).then_inc(pre_full, 16)
                sp.dma_start(freq[:, 1:2], rope_sign.rearrange("(p a) -> p a", a=1)).then_inc(pre_full, 16)
            for t in range(T):
                sp.dma_start(X[:, t, :], x[0, t * P:(t + 1) * P, :]).then_inc(start_full, 16)
            sp.dma_start(rwraw, router_w.rearrange("(p c) e -> p c e", c=DC)).then_inc(rw_full, 16)

            with sp.Fori(0, DEPTH) as l:
                first = {"u": 0, "v": 256, "cq": 512, "ckv": 768, "b": 928, "c": 1184, "h": 1440, "d": 1696}
                for u, name in enumerate(IN_UNITS):
                    n = 160 if name == "ckv" else 256
                    load(u, l, by_columns(w_in[l], first[name], n), (DC, n))
                for i in range(K_EARLY):
                    load(K_UNITS[i], l, by_columns(xattn_wk[l], 256 * i, 256), (DC, 256))
                for i, (c0, n) in enumerate(OUT_CHUNKS):
                    src = w_out[l, c0 * P:(c0 + n) * P, :].rearrange("(c p) n -> p c n", p=P)
                    load(U_OUT + i, l, src, (n, D))
                for i in range(K_EARLY, 4):
                    load(K_UNITS[i], l, by_columns(xattn_wk[l], 256 * i, 256), (DC, 256))
                for i in range(4):
                    load(U_V + i, l, xattn_wv[l].rearrange("(p c) n -> p c n", c=DC)[:, 2 * i:2 * i + 2, :], (2, D))
                for i in range(4):
                    load(U_Q + i, l, by_columns(xattn_wq[l], 256 * i, 256), (DC, 256))
                for i in range(4):
                    src = xattn_wo[l, 2 * i * P:(2 * i + 2) * P, :].rearrange("(c p) n -> p c n", p=P)
                    load(U_O + i, l, src, (2, D))
                for k in range(2):
                    expert(l, k, "g", gate_unit(k), 0)
                    expert(l, k, "u", up_unit(k), 0)
                with sp.Fori(0, STEPS) as i:
                    for k in (2, 3):
                        expert(l, i * 2 + k, "g", gate_unit(k), i * 6)
                        expert(l, i * 2 + (k - 2), "d", down_unit(k - 2), i * 6)
                        expert(l, i * 2 + k, "u", up_unit(k), i * 6)
                for k in (E - 2, E - 1):
                    expert(l, k, "d", down_unit(k), 0)
            for t in range(T):
                sp.wait_ge(x_ready, T + 3 * T * DEPTH - T + t + 1)
                sp.dma_start(out[0, t * P:(t + 1) * P, :], X[:, t, :]).then_inc(stored, 16)
            sp.wait_ge(stored, 16 * T)

        SMALL_LAYER = 16 * 17

        @block.gpsimd
        def _(pool):
            nc.gpsimd.memset(ident[:], 0.0)
            nc.gpsimd.memset(causal[:], 0.0)
            nc.gpsimd.memset(minus_half[:], -0.5)
            nc.gpsimd.memset(ones[:], 1.0)
            nc.gpsimd.memset(before[:], 1.0)
            pool.drain()
            nc.gpsimd.affine_select(out=ident[:], in_=ident[:], compare_op=ALU.not_equal, fill=1.0, base=0,
                                    pattern=[[-1, P]], channel_multiplier=1)
            nc.gpsimd.affine_select(out=causal[:], in_=causal[:], compare_op=ALU.is_ge, fill=MASKED, base=0,
                                    pattern=[[-1, P]], channel_multiplier=1)
            nc.gpsimd.affine_select(out=before[:], in_=before[:], compare_op=ALU.is_gt, fill=0.0, base=0,
                                    pattern=[[1, P]], channel_multiplier=-1)
            nc.gpsimd.iota(slots[:], pattern=[[1, P]], base=0, channel_multiplier=0,
                           allow_small_or_imprecise_dtypes=True)
            pool.drain().then_inc(ident_ready, 1)

            pool.dma_start(pinv[:], pool_inv).then_inc(const_full, 16)
            pool.dma_start(order[:], pair_order).then_inc(const_full, 16)
            pool.dma_start(rb[:], router_b.partition_broadcast(P)).then_inc(const_full, 16)

            def load_small(l):
                if l:
                    pool.wait_ge(misc_ready, misc_done("cs3", l - 1))
                with nc.allow_non_contiguous_dma(reason="small vectors, one element a partition"):
                    small = [
                        (wuq_in, mla_w_uq[l].rearrange("(c p) n -> p c n", p=P)),
                        (wukv[:], mla_w_ukv[l]),
                        (ws[:], gmlp_w_s[l].rearrange("h t s -> t h s")),
                        (vg[:], gmlp_v_norm_g[l].partition_broadcast(P)),
                        (qg[:, 0:2], mla_q_norm_g[l].rearrange("(c p) -> p c", p=P)),
                        (qg[:, 2:3], mla_kv_norm_g[l].rearrange("(p a) -> p a", a=1)),
                        (psc[:], pool_scale[l].rearrange("(c p) -> p c", p=P)),
                    ]
                    small += [(cw[:, c, :], conv_w[l][:, c * P:(c + 1) * P].rearrange("k p -> p k")) for c in range(2)]
                    small += [(pw[64 * (g % 2):64 * (g % 2) + 64, g // 2, :], pool_w[l, g]) for g in range(4)]
                    small += [(bs[64 * (h % 2):64 * (h % 2) + 64, h // 2, :], gmlp_b_s[l, h].partition_broadcast(64))
                              for h in range(A_HEADS)]
                    for dst, src in small:
                        pool.dma_start(dst, src).then_inc(small_full, 16)
                pool.dma_start(mem_in, mem[0].rearrange("(t p) d -> p t d", p=P)).then_inc(mem_full, 16)

            load_small(0)
            for l in range(DEPTH):

                def load_ln(g, b, n):
                    if n:
                        pool.wait_ge(ln_read, 2 * T * n)
                    pool.dma_start(ln_w[:, 0, :], g.partition_broadcast(P)).then_inc(ln_full, 16)
                    pool.dma_start(ln_w[:, 1, :], b.partition_broadcast(P)).then_inc(ln_full, 16)

                def ln_power(n):
                    for t in range(T):
                        if t == 0:
                            pool.wait_ge(ln_var, n + 1)
                        else:
                            pool.wait_ge(ln_stats, n + 1)
                            nc.gpsimd.tensor_scalar(lv[:, 1:2], about_mean[:], 1.0 / D, EPS, ALU.mult, ALU.add)
                            pool.drain()
                        nc.gpsimd.tensor_tensor(lr[:, t:t + 1], lv[:, t:t + 1], minus_half[:, 0:1],
                                                ALU.pow).then_inc(ln_rstd, 1)

                load_ln(ln1_g[l], ln1_b[l], 3 * l)
                pool.wait_ge(small_full, SMALL_LAYER * (l + 1))
                nc.gpsimd.affine_select(out=ws[:], in_=ws[:], compare_op=ALU.is_ge, fill=0.0, base=0,
                                        pattern=[[0, A_HEADS], [-1, CHUNK]],
                                        channel_multiplier=1).then_inc(ws_masked, 1)
                pool.wait_ge(ms_ready, l + 1)
                nc.gpsimd.tensor_tensor(rs[:], ms[:], minus_half[:], ALU.pow).then_inc(rs_ready, 1)
                pool.wait_ge(vms_ready, l + 1)
                nc.gpsimd.tensor_tensor(vrs[:], vms[:], minus_half[:, 0:2], ALU.pow).then_inc(vrs_ready, 1)
                ln_power(3 * l)
                load_ln(ln2_g[l], ln2_b[l], 3 * l + 1)
                ln_power(3 * l + 1)
                load_ln(ln3_g[l], ln3_b[l], 3 * l + 2)
                pool.wait_ge(xn_hi_done, l + 1)
                for t in range(T):
                    nc.gpsimd.tensor_tensor(xn_lo[:, t], X[:, t, :].rearrange("p (q c) -> p c q", c=DC),
                                            xn_hi[:, t].bitcast(F32), ALU.subtract)
                pool.drain().then_inc(xn_lo_done, 1)
                if l + 1 < DEPTH:
                    load_small(l + 1)
                ln_power(3 * l + 2)

        DVE_AHEAD = DVE_LAYER - 2 * E + PRO

        @block.scalar
        def _(act):
            def hi(u, l, n, i=0):
                turns = l * (UNITS // RAW_SLOTS * 16) + (u // RAW_SLOTS + 1) * 16
                if not isinstance(i, int):
                    turns = turns + i * 16
                act.wait_ge(raw_full[u % RAW_SLOTS], turns)
                act.wait_ge(unit_used, used(slot_before(u), l) + (i * 6 if not isinstance(i, int) else 0))
                for a in range(2):
                    s = slice(a * n // 2, (a + 1) * n // 2)
                    nc.scalar.copy(unit_slot(u, 0, n)[:, s], raw[:, u % RAW_SLOTS, s]).then_inc(hi_done, 1)

            def hi_rotary(l):
                act.wait_ge(raw_full[1], l * (UNITS // RAW_SLOTS * 16) + 16)
                act.wait_ge(unit_used, used(1 - SPLIT_SLOTS, l))
                h, r = kv_views(w_hi)
                for d, sl in KV_PIECES:
                    nc.scalar.copy(h[:, :, d], r[:, :, sl])
                act.drain().then_inc(hi_done, 1)
                act.drain().then_inc(hi_done, 1)

            def move(name, l, dst, src, scale=1.0, unit=None):
                if unit is None:
                    act.wait_ge(misc_ready, misc_done(name, l))
                else:
                    act.wait_ge(unit_used, used(unit, l))
                nc.scalar.activation(dst, src, ACT.Copy, scale=scale).then_inc(act_emptied, 1)

            def x_high(name, l):
                for j in range(4):
                    act.wait_ge(misc_ready, misc_done(f"{name}{j}", l))
                    t, c = j // 2, 4 * (j % 2)
                    nc.scalar.copy(x_hi[:, c:c + 4, t * P:(t + 1) * P],
                                   bank(f"{name}{j}").rearrange("p (a b) -> p a b", a=4)).then_inc(xhi_done, 1)

            def exps(h, l):
                act.wait_ge(max_ready, l * MLA_HEADS + (h + 1))
                if h >= 4:
                    act.wait_ge(misc_ready, misc_done(f"pt{h - 4}", l))
                p = bank(f"s{h}")
                nc.scalar.activation(probs[:, h % 4, 0:128], p[:, 0:128], ACT.Exp, bias=smax[:, h, 0:1],
                                     accum_out=ssum[:, h, 0:1])
                nc.scalar.activation(probs[:, h % 4, 128:384], p[:, 128:384], ACT.Exp, bias=smax[:, h, 1:2],
                                     accum_out=ssum[:, h, 1:2])
                act.drain().then_inc(act_emptied, 1)

            def probs_t(h, l):
                if h >= 2:
                    act.wait_ge(misc_ready, misc_done(f"pv{h // 2 - 1}", l))
                move(f"pt{h}", l, probsT[:, h % 2, :], bank(f"pt{h}")[:, 0:384])

            def gelu_t(n, l):
                act.wait_ge(gelu_arg, l * 2 + (n + 1))
                nc.scalar.activation(th, gt, ACT.Tanh, scale=GELU_SCALE).then_inc(gelu_tanh, 1)

            act.wait_ge(start_full, 16 * T)
            act.sem_inc(x_ready, T)
            def norm_stats(n, l):
                act.wait_ge(ln_sum, l * 3 + (n + 1))
                nc.scalar.activation(passed, X[:, 1, :], ACT.Copy, scale=-1.0 / D, accum_out=minus_mean[:])
                act.drain()
                nc.scalar.activation(passed, X[:, 1, :], ACT.Square, bias=minus_mean[:], accum_out=about_mean[:])
                act.drain().then_inc(ln_stats, 1)

            act.wait_ge(rope_arg, 1)
            nc.scalar.activation(rope_cos[:], ang[:, 2, :], ACT.Sin)
            nc.scalar.activation(rope_sin[:], ang[:, 3, :], ACT.Sin)
            act.drain().then_inc(rope_sined, 1)
            act.wait_ge(rw_full, 16)
            nc.scalar.copy(rw_hi, rwraw).then_inc(rwhi, 1)

            NORMAL = 2048
            size = {1: DC * 160, U_OUT + 4: D, U_OUT + 5: D}

            with act.Fori(0, DEPTH) as l:
                def ahead(u):
                    hi(u + SPLIT_SLOTS, l, size.get(u + SPLIT_SLOTS, NORMAL))

                hi(0, l, NORMAL)
                x_high("xa", l)
                hi_rotary(l)
                move("cq", l, cT[:, 0:2, :], bank2("cq"), unit=0)
                ahead(0)
                ahead(1)
                move("v", l, vz, bank2("v"), unit=2)
                ahead(2)
                gelu_t(0, l)
                move("u", l, uz, bank2("u"), unit=3)
                ahead(3)
                gelu_t(1, l)
                move("b", l, zb, bank2("b"), unit=4)
                ahead(4)
                for i in range(2):
                    move(f"qn{i}", l, qn[:, 2 * i:2 * i + 2, :], bank2(f"qn{i}"), scale=MLA_SCALE)
                for i in range(2):
                    move(f"kn{i}", l, kn[:, 2 * i:2 * i + 2, :], bank2(f"kn{i}"))
                for i in range(2):
                    move(f"vv{i}", l, vv[:, i, :], bank(f"vv{i}"))
                exps(0, l)
                exps(1, l)
                move("c", l, zc, bank2("c"), unit=5)
                ahead(5)
                exps(2, l)
                exps(3, l)
                move("wst", l, wsT[:].rearrange("p a b -> p (a b)"), bank("wst"))
                move("h", l, chp[:, :, CONV_W - 1:], bank2("h"), unit=6)
                ahead(6)
                probs_t(0, l)
                probs_t(1, l)
                exps(4, l)
                exps(5, l)
                move("d", l, pa[:, :, PAD:], bank2("d"), unit=7)
                x_high("mt", l)
                ahead(7)

                def keys(i):
                    move(f"xk{i}", l, kT[:, 2 * i:2 * i + 2, :], bank2(f"xk{i}"), unit=K_UNITS[i])
                    ahead(K_UNITS[i])

                keys(0)
                probs_t(2, l)
                probs_t(3, l)
                exps(6, l)
                exps(7, l)
                keys(1)
                probs_t(4, l)
                probs_t(5, l)
                keys(2)
                ahead(U_OUT)
                probs_t(6, l)
                probs_t(7, l)
                for u in range(U_OUT + 1, U_OUT + len(OUT_CHUNKS)):
                    ahead(u)
                keys(3)
                norm_stats(0, l)
                for i in range(3):
                    ahead(U_V + i)
                x_high("xb", l)
                ahead(U_V + 3)
                for t in range(T):
                    for a in range(2):
                        last = nc.scalar.copy(xv[:, t, 512 * a:512 * a + 512], quad[:, 2 * t + a, :])
                last.then_inc(values_moved, 1)
                for i in range(4):
                    move(f"xq{i}", l, qT[:, 2 * i:2 * i + 2, :], bank2(f"xq{i}"), scale=256.0 ** -0.5, unit=U_Q + i)
                    ahead(U_Q + i)
                for h in range(X_HEADS):
                    act.wait_ge(xmax_ready, l * X_HEADS + (h + 1))
                    for t in range(T):
                        nc.scalar.activation(xprobs[:, h, 256 * t:256 * t + 256],
                                             bank(f"cs{h}")[:, 256 * t:256 * t + 256], ACT.Exp,
                                             bias=smax[:, h, t:t + 1], accum_out=ssum[:, h, t:t + 1])
                    act.drain().then_inc(act_emptied, 1)
                def x_probs_t(h):
                    if h >= 2:
                        act.wait_ge(misc_ready, misc_done(f"cpv{h - 2}", l))
                    move(f"cpt{h}", l, xprobsT[:, h % 2, :], bank(f"cpt{h}"))

                x_probs_t(0)
                for h in range(X_HEADS):
                    if h + 1 < X_HEADS:
                        x_probs_t(h + 1)
                    move(f"cpv{h}", l, qT[:, 2 * h:2 * h + 2, :], bank2(f"cpv{h}"))
                ahead(U_O)
                ahead(U_O + 1)
                act.wait_ge(y_ready, l * 11 + 11)
                for k in range(3):
                    hi(U_MOE + k, l, NORMAL)
                norm_stats(1, l)
                x_high("xc", l)
                move("rt0", l, logitsT, bank("rt0")[:, 0:SEQ])
                act.wait_ge(misc_ready, misc_done("rt1", l))
                nc.scalar.activation(rt[:, 1], bank("rt1")[:, 0:SEQ].rearrange("p (t e) -> p t e", t=T)[:, :, 0:E],
                                     ACT.Exp, scale=-1.0).then_inc(act_emptied, 1)
                for t in range(T):
                    last = nc.scalar.copy(xn_hi[:, t], X[:, t, :].rearrange("p (q c) -> p c q", c=DC))
                last.then_inc(xn_hi_done, 1)

                def tanh(dst, src, g_unit, i=0):
                    act.wait_ge(unit_used, used(g_unit, l) + i)
                    nc.scalar.activation(dst, src, ACT.Tanh, scale=0.5).then_inc(moe_tanh, 1)

                act.wait_ge(fits_ready, l + 1)
                act.sem_inc(act_passed, 1)
                with act.If(act.value_load(fits[0:1, 0:1], min_val=0, max_val=1)):
                    act.sem_inc(act_emptied, 8)

                    def gather_high(pair):
                        for r in range(4):
                            act.wait_ge(gathered, l * 8 + (4 * pair + r + 1))
                            nc.scalar.copy(x_hi[:, 2 * r:2 * r + 2, :],
                                           gather_bank(pair, r).rearrange("p (a b) -> p a b", a=2)).then_inc(gath_hi, 1)

                    def turned_high(k):
                        act.wait_ge(turned, l * E + (k + 1))
                        nc.scalar.copy(y_hi[:, k % 2, :], ring[:, 1, FF:2 * FF]).then_inc(turned_hi, 1)

                    def out_high(g):
                        act.wait_ge(half_out, l * N_GROUPS + (g + 1))
                        for a in range(2):
                            if a:
                                act.wait_ge(unit_used, used(down_unit(PER_GROUP * g + PER_GROUP - 1), l))
                            nc.scalar.copy(y_hi[:, 2 + 2 * a:4 + 2 * a, :],
                                           ring[:, 2 + a, :].rearrange("p (a b) -> p a b", a=2)).then_inc(out_hi, 1)

                    gather_high(0)
                    tanh(s_th[:, 0, :], ring[:, 0, 0:FF], gate_unit(0))
                    act.wait_ge(to_token_done, l + 1)
                    for a in range(2):
                        last = nc.scalar.copy(to_token[:, 2 * a:2 * a + 2, :],
                                              ring[:, 2 + a, :].rearrange("p (a b) -> p a b", a=2))
                    last.then_inc(to_token_moved, 1)
                    for k in range(1, E):
                        if k == E // 2:
                            gather_high(1)
                        hi(up_unit(k), l, NORMAL)
                        tanh(s_th[:, k % 2, :], ring[:, 0, 0:FF], gate_unit(k))
                        turned_high(k - 1)
                        hi(up_unit(k) + 1, l, NORMAL)
                        if k >= 5 and k % PER_GROUP == 1:
                            out_high(k // PER_GROUP - 1)
                        hi(up_unit(k) + 2, l, NORMAL)
                    turned_high(E - 1)
                    out_high(N_GROUPS - 1)
                with act.Else():
                    act.wait_ge(xn_lo_done, l + 1)
                    for i in range(8):
                        move(f"gb{i}", l, gbc[:, 2 * i:2 * i + 2, :], bank2(f"gb{i}"), scale=0.5)
                    tanh(m_th, ring[:, 0, :], gate_unit(0))

                    def step(k, i, e):
                        hi(up_unit(k), l, NORMAL, i)
                        act.wait_ge(dve_emptied, l * DVE_LAYER + e * 2 + (DVE_AHEAD + 2 * k - 1))
                        tanh(m_th, ring[:, 2 * (k % 2), :], gate_unit(k), i if isinstance(i, int) else i * 6)
                        hi(up_unit(k) + 1, l, NORMAL, i)
                        hi(up_unit(k) + 2, l, NORMAL, i)

                    step(1, 0, 0)
                    with act.Fori(0, STEPS) as i:
                        step(2, i, i * 2)
                        step(3, i, i * 2)
                    act.sem_inc(gath_hi, 8)
                    act.sem_inc(to_token_moved, 1)
                    act.sem_inc(turned_hi, E)
                    act.sem_inc(out_hi, 2 * N_GROUPS)
                norm_stats(2, l)

        @block.vector
        def _(dve):
            def lo(u, l, n, i=0):
                for a in range(2):
                    c = l * (2 * UNITS) + (2 * u + a + 1)
                    dve.wait_ge(hi_done, c + i * 12 if not isinstance(i, int) else c)
                    s = slice(a * n // 2, (a + 1) * n // 2)
                    last = nc.vector.tensor_tensor(unit_slot(u, 1, n)[:, s], raw[:, u % RAW_SLOTS, s],
                                                   unit_slot(u, 0, n)[:, s].bitcast(F32), ALU.subtract)
                last.then_inc(split_done, 1)

            def lo_rotary(l):
                dve.wait_ge(hi_done, l * (2 * UNITS) + 4)
                w, r = kv_views(w_lo)
                h, _ = kv_views(w_hi)
                for d, sl in KV_PIECES:
                    nc.vector.tensor_tensor(w[:, :, d], r[:, :, sl], h[:, :, d].bitcast(F32), ALU.subtract)
                dve.drain().then_inc(split_done, 1)

            def x_low(name, l, n, halfway=None):
                for j in range(4):
                    if j == 2 and halfway:
                        halfway()
                    dve.wait_ge(xhi_done, l * 16 + (4 * n + j + 1))
                    t, c = j // 2, 4 * (j % 2)
                    s = (slice(None), slice(c, c + 4), slice(t * P, (t + 1) * P))
                    nc.vector.tensor_tensor(x_lo[s], bank(f"{name}{j}").rearrange("p (a b) -> p a b", a=4),
                                            x_hi[s].bitcast(F32), ALU.subtract).then_inc(dve_emptied, 1)

            def split_y(c, n, src):
                nc.vector.tensor_copy(y_hi[:, c:c + n, :], src)
                dve.drain()
                nc.vector.tensor_tensor(y_lo[:, c:c + n, :], src, y_hi[:, c:c + n, :].bitcast(F32),
                                        ALU.subtract).then_inc(y_ready, 1)
                dve.drain()

            def gelu_poly(z):
                nc.vector.tensor_tensor(gt, z, z, ALU.mult)
                dve.drain()
                nc.vector.tensor_scalar(gt, gt, GELU_CUBIC, 1.0, ALU.mult, ALU.add)
                dve.drain()
                nc.vector.tensor_tensor(gt, gt, z, ALU.mult).then_inc(gelu_arg, 1)

            def gelu_end(z, n, l):
                dve.wait_ge(gelu_tanh, l * 2 + (n + 1))
                nc.vector.scalar_tensor_tensor(z, th, 1.0, z, ALU.add, ALU.mult)
                dve.drain()

            def head_max(h, l):
                dve.wait_ge(misc_ready, misc_done(f"s{h}", l))
                p = bank(f"s{h}")
                b = p[:, 0:384]
                diag = bass.AP(b.tensor, b.offset, [list(b.ap[0]), [256, 2], [1, 128]])
                mask = bass.AP(causal[:].tensor, 0, [list(causal[:].ap[0]), [0, 2], [1, 128]])
                nc.vector.tensor_tensor(diag, diag, mask, ALU.add)
                dve.drain()
                nc.vector.tensor_reduce(smax[:, h, 0:1], p[:, 0:128], AX_X, ALU.max, negate=True)
                nc.vector.tensor_reduce(smax[:, h, 1:2], p[:, 128:384], AX_X, ALU.max, negate=True)
                dve.drain().then_inc(max_ready, 1)

            def head_norm(h, l):
                dve.wait_ge(act_emptied, emptied(f"s{h}", l))
                nc.vector.reciprocal(srec[:, h, :], ssum[:, h, :])
                dve.drain()
                nc.vector.tensor_scalar(probs[:, h % 4, 0:128], probs[:, h % 4, 0:128], srec[:, h, 0:1], None, ALU.mult)
                nc.vector.tensor_scalar(probs[:, h % 4, 128:384], probs[:, h % 4, 128:384], srec[:, h, 1:2], None,
                                        ALU.mult)
                dve.drain().then_inc(probs_ready, 1)

            def layer_norm(n, l, done, count, meanwhile=(None, None)):
                def add(t):
                    for a in range(2):
                        s = slice(512 * a, 512 * a + 512)
                        nc.vector.scalar_tensor_tensor(X[:, t, s], X[:, t, s], ALPHA, quad[:, 2 * t + a, :],
                                                       ALU.mult, ALU.add)
                    dve.drain().then_inc(quad_free, 1)
                    if t:
                        dve.sem_inc(ln_sum, 1)

                def stats(t):
                    for a in range(2):
                        nc.vector.bn_stats(bn[:, t, a, :], X[:, t, 512 * a:512 * a + 512])
                    dve.drain()
                    nc.vector.bn_aggr(mv[:, t, :], bn[:, t].rearrange("p a b -> p (a b)"))
                    dve.drain()
                    nc.vector.tensor_scalar(lv[:, t:t + 1], mv[:, t, 1:2], EPS, None,
                                            ALU.add).then_inc(ln_var, 1)

                def affine(t):
                    dve.wait_ge(ln_rstd, l * (3 * T) + (n * T + t + 1))
                    mean, op = (minus_mean[:], ALU.add) if t else (mv[:, t, 0:1], ALU.subtract)
                    nc.vector.scalar_tensor_tensor(X[:, t, :], X[:, t, :], mean, ln_w[:, 0, :],
                                                   op, ALU.mult).then_inc(ln_read, 1)
                    dve.drain()
                    nc.vector.scalar_tensor_tensor(X[:, t, :], X[:, t, :], lr[:, t:t + 1], ln_w[:, 1, :],
                                                   ALU.mult, ALU.add).then_inc(ln_read, 1)
                    dve.drain().then_inc(x_ready, 1)

                dve.wait_ge(quad_ready, l * 3 + (n + 1))
                add(0)
                stats(0)
                dve.wait_ge(done, count)
                add(1)
                if meanwhile[0]:
                    meanwhile[0]()
                dve.wait_ge(ln_full, l * 96 + 32 * (n + 1))
                affine(0)
                if meanwhile[1]:
                    meanwhile[1]()
                affine(1)

            dve.sem_inc(split_done, RAW_SLOTS)
            dve.sem_inc(dve_emptied, PRO)

            dve.wait_ge(pre_full, 16 * 3)
            a0, a1, a2, a3 = (ang[:, i, :] for i in range(4))
            nc.vector.tensor_copy(a0, pos_i.bitcast(I32))
            dve.drain()
            nc.vector.tensor_scalar(a0, a0, freq[:, 0:1], None, ALU.mult)
            dve.drain()
            nc.vector.tensor_scalar(a1, a0, 1.0 / TWO_PI, None, ALU.mult)
            dve.drain()
            nc.vector.tensor_scalar(a1, a1, ROUND_MAGIC, None, ALU.add)
            dve.drain()
            nc.vector.tensor_scalar(a1, a1, ROUND_MAGIC, None, ALU.subtract)
            dve.drain()
            for part in (TURN_HI, TURN_MID, TURN_LO):
                nc.vector.scalar_tensor_tensor(a0, a1, -part, a0, ALU.mult, ALU.add)
                dve.drain()
            nc.vector.tensor_scalar(a3, a0, PI_BELOW, -PI_BELOW, ALU.min, ALU.max)
            nc.vector.tensor_scalar(a1, a0, -1.0, None, ALU.mult)
            dve.drain()
            nc.vector.tensor_tensor(a2, a0, a1, ALU.max)
            dve.drain()
            nc.vector.tensor_scalar(a2, a2, -1.0, float(np.pi / 2), ALU.mult, ALU.add)
            dve.drain().then_inc(rope_arg, 1)
            dve.wait_ge(rope_sined, 1)
            nc.vector.tensor_scalar(rope_sin[:], rope_sin[:], freq[:, 1:2], None, ALU.mult)
            dve.wait_ge(rwhi, 1)
            nc.vector.tensor_tensor(rw_lo, rwraw, rw_hi.bitcast(F32), ALU.subtract)
            nc.vector.memset(rw[:, 2 * P:].bitcast(F32), 0.0)
            dve.drain()
            NORMAL = 2048
            size = {1: DC * 160, U_OUT + 4: D, U_OUT + 5: D}

            with dve.Fori(0, DEPTH) as l:
                def split_pair(i):
                    dve.wait_ge(misc_ready, misc_done(f"pv{i}", l))
                    src = bank(f"pv{i}")[:, 0:SEQ]
                    nc.vector.tensor_copy(y_hi[:, 2 + i, :], src)
                    dve.drain()
                    nc.vector.tensor_tensor(y_lo[:, 2 + i, :], src, y_hi[:, 2 + i, :].bitcast(F32), ALU.subtract)
                    dve.drain().then_inc(dve_emptied, 1)
                    dve.drain().then_inc(y_ready, 1)

                def ahead(u):
                    lo(u + SPLIT_SLOTS, l, size.get(u + SPLIT_SLOTS, NORMAL))

                lo(0, l, NORMAL)
                x_low("xa", l, 0)
                lo_rotary(l)
                dve.wait_ge(act_emptied, emptied("cq", l))
                nc.vector.tensor_tensor(sq[:, 0:2, :], cT[:, 0:2, :], cT[:, 0:2, :], ALU.mult).then_inc(sq_ready, 1)
                ahead(0)
                dve.wait_ge(unit_used, used(1, l))
                kvb = bank("ckv")
                nc.vector.tensor_copy(cT[:, 2, :], kvb[:, 0:SEQ])
                nc.vector.tensor_tensor(kr[0:32], kvb[64:96, SEQ:], rope_cos[64:96], ALU.mult)
                nc.vector.tensor_tensor(rtmp[0:32, 0, :], kvb[96:128, SEQ:], rope_sin[96:128], ALU.mult)
                dve.drain().then_inc(dve_emptied, 1)
                nc.vector.tensor_tensor(sq[:, 2, :], cT[:, 2, :], cT[:, 2, :], ALU.mult).then_inc(sq_ready, 1)
                nc.vector.tensor_tensor(kr[0:32], kr[0:32], rtmp[0:32, 0, :], ALU.add)
                dve.drain()
                for g in range(1, 4):
                    nc.vector.tensor_copy(kr[32 * g:32 * g + 32], kr[0:32])
                dve.drain()
                ahead(1)
                dve.wait_ge(act_emptied, emptied("v", l))
                gelu_poly(vz)
                dve.wait_ge(misc_ready, misc_done("ssq", l))
                nc.vector.tensor_scalar(ms[:, 0:2], bank("ssq")[:, 0:2], 1.0 / QL, EPS, ALU.mult,
                                        ALU.add).then_inc(dve_emptied, 1)
                dve.wait_ge(misc_ready, misc_done("ssk", l))
                nc.vector.tensor_scalar(ms[:, 2:4], bank("ssk")[:, 0:2], 1.0 / P, EPS, ALU.mult,
                                        ALU.add).then_inc(dve_emptied, 1)
                dve.drain().then_inc(ms_ready, 1)
                dve.wait_ge(small_full, l * SMALL_LAYER + SMALL_LAYER)
                for c in range(2):
                    src = wuq_in[:, c, :].rearrange("p (h n) -> p h n", h=MLA_HEADS)
                    rope = wuq[c][:, 512:768].rearrange("p (h n) -> p h n", h=MLA_HEADS)
                    swap = wuq[c][:, 768:1024].rearrange("p (h n) -> p h n", h=MLA_HEADS)
                    nc.vector.tensor_copy(wuq[c][:, 0:512].rearrange("p (h n) -> p h n", h=MLA_HEADS), src[:, :, 0:NOPE])
                    nc.vector.tensor_copy(rope, src[:, :, NOPE:])
                    nc.vector.tensor_copy(swap[:, :, 0:16], src[:, :, NOPE + 16:])
                    nc.vector.tensor_copy(swap[:, :, 16:32], src[:, :, NOPE:NOPE + 16])
                dve.drain().then_inc(wuq_ready, 1)
                nc.vector.memset(chp[:, :, 0:CONV_W - 1], 0.0)
                nc.vector.memset(pa[:, :, 0:PAD], 0.0)
                nc.vector.memset(pb_[:, :, 0:1], 0.0)
                nc.vector.memset(pc[:, :, 0:2], 0.0)
                ahead(2)
                gelu_end(vz, 0, l)
                for t in range(T):
                    nc.vector.tensor_tensor_reduce(out=gt[:, t, :], in0=vz[:, t, :], in1=vz[:, t, :],
                                                   scale=0.25 / 256, scalar=EPS, op0=ALU.mult, op1=ALU.add,
                                                   accum_out=vms[:, t:t + 1])
                dve.drain().then_inc(vms_ready, 1)
                dve.wait_ge(act_emptied, emptied("u", l))
                gelu_poly(uz)
                dve.wait_ge(vrs_ready, l + 1)
                nc.vector.tensor_scalar(vrs[:], vrs[:], 0.5, None, ALU.mult)
                dve.drain()
                for t in range(T):
                    nc.vector.scalar_tensor_tensor(vz[:, t, :], vz[:, t, :], vrs[:, t:t + 1], vg[:], ALU.mult, ALU.mult)
                dve.drain().then_inc(v_ready, 1)
                dve.wait_ge(misc_ready, misc_done("rb0", l))
                for c in range(3):
                    nc.vector.scalar_tensor_tensor(cn[:, c, :], cT[:, c, :], qg[:, c:c + 1], bank2("rb0")[:, c // 2, :],
                                                   ALU.mult, ALU.mult)
                dve.drain().then_inc(dve_emptied, 1)
                ahead(3)
                gelu_end(uz, 1, l)
                ahead(4)
                cos2 = bass.AP(rope_cos[:].tensor, 0, [list(rope_cos[:].ap[0]), [0, 2], [1, SEQ]])
                sin2 = bass.AP(rope_sin[:].tensor, 0, [list(rope_sin[:].ap[0]), [0, 2], [1, SEQ]])
                dve.wait_ge(misc_ready, misc_done("qr", l))
                nc.vector.scalar_tensor_tensor(qr, bank2("qr"), MLA_SCALE, cos2, ALU.mult, ALU.mult).then_inc(dve_emptied, 1)
                dve.wait_ge(misc_ready, misc_done("qrs", l))
                nc.vector.scalar_tensor_tensor(rtmp, bank2("qrs"), MLA_SCALE, sin2, ALU.mult,
                                               ALU.mult).then_inc(dve_emptied, 1)
                dve.drain()
                nc.vector.tensor_tensor(qr, qr, rtmp, ALU.add)
                dve.drain().then_inc(rope_ready, 1)
                head_max(0, l)
                head_max(1, l)
                ahead(5)
                head_max(2, l)
                head_max(3, l)
                head_norm(0, l)
                head_norm(1, l)
                dve.wait_ge(act_emptied, emptied("h", l))
                nc.vector.tensor_tensor(chp[:, :, CONV_W - 1:], chp[:, :, CONV_W - 1:], zc, ALU.mult)
                dve.drain()
                ahead(6)
                for c in range(2):
                    nc.vector.tensor_scalar(zc[:, c, :], chp[:, c, 0:SEQ], cw[:, c, 0:1], None, ALU.mult)
                dve.drain()
                head_norm(2, l)
                head_norm(3, l)
                head_max(4, l)
                head_max(5, l)
                for k in range(1, CONV_W):
                    for c in range(2):
                        nc.vector.scalar_tensor_tensor(zc[:, c, :], chp[:, c, k:k + SEQ], cw[:, c, k:k + 1], zc[:, c, :],
                                                       ALU.mult, ALU.add)
                    dve.drain()
                nc.vector.tensor_tensor(zc, zc, zb, ALU.mult)
                dve.drain()
                split_y(6, 2, zc)
                x_low("mt", l, 1)
                ahead(7)
                split_pair(0)
                dve.wait_ge(const_full, 48)
                dve.wait_ge(act_emptied, emptied("d", l))
                W = PAD + SEQ
                nc.vector.tensor_tensor(pb_[:, :, 1:], pa[:, :, 1:], pa[:, :, 0:W - 1], ALU.add)
                dve.drain()
                nc.vector.tensor_tensor(pc[:, :, 2:], pb_[:, :, 2:], pb_[:, :, 0:W - 2], ALU.add)
                dve.drain()
                nc.vector.tensor_tensor(pb_[:, 1, 4:], pc[:, 1, 4:], pc[:, 1, 0:W - 4], ALU.add)
                dve.drain()
                nc.vector.tensor_tensor(pc[64:, 1, 8:], pb_[64:, 1, 8:], pb_[64:, 1, 0:W - 8], ALU.add)
                dve.drain()
                halves = ((slice(0, 64), 0, pb_), (slice(64, P), 0, pc), (slice(0, 64), 1, pb_), (slice(64, P), 1, pc))
                for rows, c, s in halves:
                    nc.vector.tensor_tensor(s[rows, c, PAD:2 * PAD], s[rows, c, PAD:2 * PAD], pinv[rows, c, 1:], ALU.mult)
                dve.drain()
                for rows, c, s in halves:
                    nc.vector.scalar_tensor_tensor(gt[rows, c, :], s[rows, c, PAD:], pinv[rows, c, 0:1],
                                                   pa[rows, c, PAD:], ALU.mult, ALU.subtract)
                dve.drain().then_inc(pooled, 1)
                dve.wait_ge(misc_ready, misc_done("mix", l))
                bs2 = bass.AP(bs[:].tensor, 0, [list(bs[:].ap[0]), [CHUNK, 2], [0, T], [1, CHUNK]])
                g4 = vz.rearrange("p a (t n) -> p a t n", t=T)
                nc.vector.tensor_tensor(g4, bank2("mix").rearrange("p a (t n) -> p a t n", t=T), bs2, ALU.add)
                dve.drain().then_inc(dve_emptied, 1)
                nc.vector.scalar_tensor_tensor(vz, vz, 0.5, uz, ALU.mult, ALU.mult)
                dve.drain()
                split_y(0, 2, vz)
                head_norm(4, l)
                head_norm(5, l)
                ahead(8)
                head_max(6, l)
                head_max(7, l)
                ahead(9)
                head_norm(6, l)
                head_norm(7, l)
                split_pair(1)
                ahead(10)
                dve.wait_ge(misc_ready, misc_done("yd", l))
                for c in range(2):
                    nc.vector.tensor_scalar(th[:, c, :], bank2("yd")[:, c, :], psc[:, c:c + 1], None, ALU.mult)
                dve.drain().then_inc(dve_emptied, 1)
                split_y(8, 2, th)
                split_pair(2)
                ahead(U_OUT)
                split_pair(3)
                for u in range(U_OUT + 1, U_K_LATE - 1):
                    ahead(u)
                layer_norm(0, l, unit_used, used(U_K_LATE - 1, l),
                           (lambda: (ahead(U_K_LATE - 1), ahead(U_K_LATE)), lambda: ahead(U_V)))
                for u in range(U_V + 1, U_V + 3):
                    ahead(u)
                x_low("xb", l, 2)
                ahead(U_V + 3)
                for i in range(4):
                    ahead(U_Q + i)
                for h in range(X_HEADS):
                    dve.wait_ge(misc_ready, misc_done(f"cs{h}", l))
                    nc.vector.tensor_reduce(smax[:, h, :], bank2(f"cs{h}"), AX_X, ALU.max, negate=True)
                    dve.drain().then_inc(xmax_ready, 1)
                for h in range(X_HEADS):
                    dve.wait_ge(act_emptied, emptied(f"cs{h}", l))
                    nc.vector.reciprocal(srec[:, h, :], ssum[:, h, :])
                    dve.drain()
                    for t in range(T):
                        nc.vector.tensor_scalar(xprobs[:, h, 256 * t:256 * t + 256], xprobs[:, h, 256 * t:256 * t + 256],
                                                srec[:, h, t:t + 1], None, ALU.mult)
                    dve.drain().then_inc(xprobs_ready, 1)
                for h in range(X_HEADS):
                    dve.wait_ge(act_emptied, emptied(f"cpv{h}", l))
                    split_y(2 * h, 2, qT[:, 2 * h:2 * h + 2, :])
                for i in range(2):
                    ahead(U_O + i)
                lo(U_MOE, l, NORMAL)
                layer_norm(1, l, unit_used, used(U_O + 3, l))
                x_low("xc", l, 3)
                lo(U_MOE + 1, l, NORMAL)
                lo(U_MOE + 2, l, NORMAL)

                dve.wait_ge(act_emptied, emptied("rt1", l))
                score, sel, rank, weight, grp = (rt[:, i] for i in range(1, 6))
                nc.vector.tensor_scalar(score, score, 1.0, None, ALU.add)
                dve.drain()
                nc.vector.reciprocal(score, score)
                dve.drain()
                rbb = bass.AP(rb[:].tensor, 0, [list(rb[:].ap[0]), [0, T], [1, E]])
                nc.vector.tensor_tensor(sel, score, rbb, ALU.add)
                dve.drain()

                def view(v, dims):
                    return bass.AP(v.tensor, v.offset, [list(v.ap[0])] + dims)

                def ranks(v, r, n):
                    N = PER_GROUP
                    a, b = (c[:, 0:n, :].rearrange("p g (k j) -> p g k j", k=N) for c in (precede, precede2))
                    other, own = view(v, [[N, n], [0, N], [1, N]]), view(v, [[N, n], [1, N], [0, N]])
                    is_ahead = bass.AP(order[:].tensor, 0, [list(order[:].ap[0]), [0, n], [N, N], [1, N]])
                    nc.vector.tensor_tensor(a, other, own, ALU.is_equal)
                    nc.vector.tensor_tensor(b, other, own, ALU.is_gt)
                    dve.drain()
                    nc.vector.tensor_tensor(a, a, is_ahead, ALU.mult)
                    dve.drain()
                    nc.vector.tensor_tensor(a, a, b, ALU.add)
                    dve.drain()
                    nc.vector.tensor_reduce(r, a, AX_X, ALU.add)
                    dve.drain()

                group_score, group_rank = grp[:, 0, 0:8], grp[:, 1, 0:8]
                grv = group_rank.rearrange("p (t g) -> p t g", t=T)
                four = [[PER_GROUP, 8], [1, PER_GROUP]]
                ranks(sel, view(rank, four), 8)
                nc.vector.scalar_tensor_tensor(weight, rank, 2.0, sel, ALU.is_lt, ALU.mult)
                dve.drain()
                nc.vector.tensor_reduce(group_score, view(weight, four), AX_X, ALU.add)
                dve.drain()
                ranks(group_score, view(group_rank, [[N_GROUPS, T], [1, N_GROUPS]]), T)
                nc.vector.tensor_scalar(group_rank, group_rank, 1.0, None, ALU.is_lt)
                nc.vector.scalar_tensor_tensor(weight, rank, 2.0, score, ALU.is_lt, ALU.mult)
                dve.drain().then_inc(member_ready, 1)
                nc.vector.tensor_tensor(view(weight, four), view(weight, four), view(group_rank, [[1, 8], [0, PER_GROUP]]),
                                        ALU.mult)
                dve.drain()
                nc.vector.tensor_reduce(grp[:, 0, 8:10], weight, AX_X, ALU.add)
                dve.drain()
                nc.vector.reciprocal(grp[:, 0, 10:12], grp[:, 0, 8:10])
                dve.drain()
                nc.vector.tensor_tensor(gates[:], weight, view(grp[:, 0, 10:12], [[1, T], [0, E]]), ALU.mult)
                dve.drain().then_inc(gates_ready, 1)

                dve.wait_ge(placed, l + 1)
                counts = bank("rt0")[:, 256:256 + 3 * N_GROUPS]
                nc.vector.tensor_copy(place[:].rearrange("p t g -> p (t g)"), counts[:, 0:T * N_GROUPS])
                nc.vector.tensor_reduce(grp[:, 0, 12:13], counts[:, T * N_GROUPS:], AX_X, ALU.max)
                dve.drain()
                nc.vector.tensor_scalar(fits[:], grp[:, 0, 12:13], float(P), None, ALU.is_le)
                dve.drain().then_inc(fits_ready, 1)
                for g in range(N_GROUPS):
                    for t in range(T):
                        nc.vector.tensor_scalar(to_slot(t)[:, g * P:(g + 1) * P], slots[:], place[:, t, g:g + 1],
                                                grv[:, t, g:g + 1], ALU.is_equal, ALU.mult)
                    if g % 2:
                        dve.drain().then_inc(slots_ready, 1)

                with dve.If(dve.value_load(fits[0:1, 0:1], min_val=0, max_val=1)):
                    def gather_low(pair):
                        for r in range(4):
                            dve.wait_ge(gath_hi, l * 8 + (4 * pair + r + 1))
                            nc.vector.tensor_tensor(x_lo[:, 2 * r:2 * r + 2, :],
                                                    gather_bank(pair, r).rearrange("p (a b) -> p a b", a=2),
                                                    x_hi[:, 2 * r:2 * r + 2, :].bitcast(F32),
                                                    ALU.subtract).then_inc(gath_lo, 1)

                    def gated(k):
                        dve.wait_ge(moe_tanh, l * E + (k + 1))
                        nc.vector.scalar_tensor_tensor(s_t[:, k % 2, :], s_th[:, k % 2, :], 1.0, ring[:, 0, 0:FF],
                                                       ALU.add, ALU.mult).then_inc(dve_emptied, 1)

                    def times_up(k):
                        dve.drain()
                        dve.wait_ge(unit_used, used(up_unit(k), l))
                        nc.vector.scalar_tensor_tensor(s_t[:, k % 2, :], s_t[:, k % 2, :], slot_gates[:, k:k + 1],
                                                       ring[:, 1, 0:FF], ALU.mult, ALU.mult).then_inc(dve_emptied, 1)

                    def turned_low(k):
                        dve.wait_ge(turned_hi, l * E + (k + 1))
                        nc.vector.tensor_tensor(y_lo[:, k % 2, :], ring[:, 1, FF:2 * FF], y_hi[:, k % 2, :].bitcast(F32),
                                                ALU.subtract).then_inc(h_ready, 1)

                    def out_low(g):
                        for a in range(2):
                            dve.wait_ge(out_hi, l * 2 * N_GROUPS + (2 * g + a + 1))
                            last = nc.vector.tensor_tensor(y_lo[:, 2 + 2 * a:4 + 2 * a, :],
                                                           ring[:, 2 + a, :].rearrange("p (a b) -> p a b", a=2),
                                                           y_hi[:, 2 + 2 * a:4 + 2 * a, :].bitcast(F32), ALU.subtract)
                        last.then_inc(out_split, 1)

                    gather_low(0)
                    dve.wait_ge(slot_gated, l + 1)
                    nc.vector.tensor_scalar(slot_gates[:], quad[:, 0, 0:E], 0.5, None, ALU.mult)
                    gated(0)
                    for k in range(1, E):
                        times_up(k - 1)
                        if k == E // 2:
                            gather_low(1)
                        lo(up_unit(k), l, NORMAL)
                        gated(k)
                        turned_low(k - 1)
                        lo(up_unit(k) + 1, l, NORMAL)
                        if k >= 5 and k % PER_GROUP == 1:
                            out_low(k // PER_GROUP - 1)
                        if k == E - 1:
                            times_up(k)
                        lo(up_unit(k) + 2, l, NORMAL)
                    turned_low(E - 1)
                    out_low(N_GROUPS - 1)
                with dve.Else():
                    def hidden(par, gates_of, u, i, e):
                        t = m_t[:, par, :]
                        dve.wait_ge(moe_tanh, l * E + (e + 1))
                        nc.vector.scalar_tensor_tensor(t, m_th, 1.0, ring[:, 2 * par, :], ALU.add,
                                                       ALU.mult).then_inc(dve_emptied, 1)
                        dve.drain()
                        dve.wait_ge(unit_used, used(u, l) + i)
                        nc.vector.tensor_tensor(t, t, ring[:, 2 * par + 1, :], ALU.mult).then_inc(dve_emptied, 1)
                        dve.drain()
                        t2 = t.rearrange("p (a b) -> p a b", a=2)
                        nc.vector.tensor_tensor(t2, t2, gates_of, ALU.mult)
                        dve.drain()
                        nc.vector.tensor_copy(y_hi[:, 2 * par:2 * par + 2, :], t2)
                        dve.drain()
                        nc.vector.tensor_tensor(y_lo[:, 2 * par:2 * par + 2, :], t2,
                                                y_hi[:, 2 * par:2 * par + 2, :].bitcast(F32),
                                                ALU.subtract).then_inc(h_ready, 1)
                        dve.drain()

                    def gate_rows(e):
                        a = gbc[:, 0, :]
                        return bass.AP(a.tensor, a.offset + e * SEQ, [list(a.ap[0]), [0, 2], [1, SEQ]])

                    def lo_step(k, i):
                        for u in range(up_unit(k), up_unit(k) + 3):
                            lo(u, l, NORMAL, i)

                    dve.wait_ge(act_emptied, emptied("gb7", l))
                    hidden(0, gate_rows(0), up_unit(0), 0, 0)
                    lo_step(1, 0)
                    hidden(1, gate_rows(1), up_unit(1), 0, 1)
                    lo_step(2, 0)
                    hidden(0, gate_rows(2), up_unit(2), 0, 2)
                    lo_step(3, 0)
                    with dve.Fori(1, STEPS) as i:
                        hidden(1, gate_rows(i * 2 + 1), up_unit(3) - 6, i * 6, i * 2 + 1)
                        lo_step(2, i)
                        hidden(0, gate_rows(i * 2 + 2), up_unit(2), i * 6, i * 2 + 2)
                        lo_step(3, i)
                    hidden(1, gate_rows(E - 1), up_unit(E - 1), 0, E - 1)
                    dve.sem_inc(gath_lo, 8)
                    dve.sem_inc(out_split, N_GROUPS)
                layer_norm(2, l, moe_done, l + 1)

        @block.tensor
        def _(pe):
            mm = nc.tensor.matmul

            def free(name, l):
                i = INDEX[name]
                if i >= 4:
                    last, by = JOBS[i - 4]
                    pe.wait_ge(act_emptied if by == "act" else dve_emptied, emptied(last, l))
                else:
                    pe.wait_ge(dve_emptied, l * DVE_LAYER + PRO)
                return bank(name)

            def three(out, a_hi, a_lo, b_hi, b_lo, first, last):
                mm(out, a_hi, b_hi, start=first, stop=False)
                mm(out, a_hi, b_lo, start=False, stop=False)
                return mm(out, a_lo, b_hi, start=False, stop=last)

            def unit_views(u, k, n):
                return (unit_slot(u, 0, k * n).rearrange("p (k n) -> p k n", k=k),
                        unit_slot(u, 1, k * n).rearrange("p (k n) -> p k n", k=k))

            def rows_out(out, u, cols, l, n=256):
                h, lw = unit_views(u, DC, n)
                for k in range(DC):
                    r = three(out, cols(h[:, k, :]), cols(lw[:, k, :]), x_hi[:, k, :], x_lo[:, k, :], k == 0, k == DC - 1)
                return r

            def project(name, u, l):
                pe.wait_ge(split_done, split(u, l))
                o = free(name, l)
                for c in range(2):
                    r = rows_out(o[:, c * SEQ:(c + 1) * SEQ], u, lambda v: v[:, c * P:(c + 1) * P], l)
                r.then_inc(unit_used, 1)

            def into_quad(a_hi, a_lo, c0, n, u, l, first, last, i=0, values=False):
                pe.wait_ge(split_done, split(u, l) + i)
                h, lw = unit_views(u, n, D)
                for t in range(T):
                    s = slice(t * P, (t + 1) * P)
                    for k in range(n):
                        for a in range(2):
                            r = three(quad[:, 2 * t + a, :], a_hi[:, c0 + k, s], a_lo[:, c0 + k, s],
                                      h[:, k, 512 * a:512 * a + 512], lw[:, k, 512 * a:512 * a + 512],
                                      first and k == 0, last and k == n - 1)
                    if last and t == 0 and not values:
                        r.then_inc(quad_ready, 1)
                r.then_inc(unit_used, 1)

            def transpose_x(name, l, n):
                for j in range(4):
                    t, c0 = j // 2, 4 * (j % 2)
                    if name == "mt":
                        pe.wait_ge(mem_full, l * 16 + 16)
                    else:
                        pe.wait_ge(x_ready, l * (3 * T) + (n * T + t + 1))
                    o = free(f"{name}{j}", l)
                    for c in range(4):
                        src = (mem_in if name == "mt" else X)[:, t, :].rearrange("p (q c) -> p c q", c=DC)[:, c0 + c, :]
                        r = nc.tensor.transpose(o[:, c * P:(c + 1) * P], src, ident[:])
                    r.then_inc(misc_ready, 1)

            pe.sem_inc(unit_used, SPLIT_SLOTS)
            pe.wait_ge(ident_ready, 1)
            pe.sem_inc(misc_ready, PRO)

            def scores(h, l):
                o = free(f"s{h}", l)
                n0, r0 = 64 * (h % 2), 32 * (h % 4)
                for t in range(T):
                    q, k = slice(t * P, (t + 1) * P), slice(0, (t + 1) * P)
                    d = o[:, 0:128] if t == 0 else o[:, 128:384]
                    mm(d, qn[n0:n0 + 64, h // 2, q], kn[n0:n0 + 64, h // 2, k], start=True, stop=False)
                    r = mm(d, qr[r0:r0 + 32, h // 4, q], kr[r0:r0 + 32, k], start=False, stop=True)
                r.then_inc(misc_ready, 1)

            def probs_t(h, l):
                pe.wait_ge(probs_ready, l * MLA_HEADS + (h + 1))
                o = free(f"pt{h}", l)
                for j, c in enumerate((0, 128, 256)):
                    r = nc.tensor.transpose(o[:, c:c + 128], probs[:, h % 4, c:c + 128], ident[:])
                r.then_inc(misc_ready, 1)

            def attend(i, l):
                o = free(f"pv{i}", l)
                pe.wait_ge(act_emptied, emptied(f"pt{2 * i + 1}", l))
                for h in (2 * i, 2 * i + 1):
                    rows = slice(64 * (h % 2), 64 * (h % 2) + 64)
                    mm(o[rows, 0:256], vv[:, 0, 64 * h:64 * h + 64], probsT[:, h % 2, 0:256], start=True, stop=False,
                       skip_group_check=True)
                    r = mm(o[rows, 128:256], vv[:, 1, 64 * h:64 * h + 64], probsT[:, h % 2, 256:384], start=False,
                           stop=True, skip_group_check=True)
                r.then_inc(misc_ready, 1)

            with pe.Fori(0, DEPTH) as l:
                transpose_x("xa", l, 0)
                pe.wait_ge(dve_emptied, emptied("xa3", l))
                project("cq", 0, l)
                pe.wait_ge(split_done, split(1, l))
                o = free("ckv", l)
                rows_out(o[:, 0:SEQ], 1, lambda v: v[:, 0:P], l, n=KV_COLS)
                rows_out(o[:, SEQ:], 1, lambda v: v[:, KV_COLS - P:], l, n=KV_COLS).then_inc(unit_used, 1)
                pe.wait_ge(split_done, split(2, l))
                o = free("v", l)
                h, lw = unit_views(2, DC, 256)
                for t in range(T):
                    s = slice(t * P, (t + 1) * P)
                    for k in range(DC):
                        r = three(o[:, t * 256:(t + 1) * 256], x_hi[:, k, s], x_lo[:, k, s], h[:, k, :], lw[:, k, :],
                                  k == 0, k == DC - 1)
                r.then_inc(unit_used, 1)
                for name, cs, n in (("ssq", (0, 1), 1), ("ssk", (2,), 2)):
                    pe.wait_ge(sq_ready, l * 2 + n)
                    o = free(name, l)
                    for t in range(T):
                        for c in cs:
                            r = mm(o[:, t:t + 1], sq[:, c, t * P:(t + 1) * P], ones[:, 0:1], start=c == cs[0],
                                   stop=c == cs[-1])
                    r.then_inc(misc_ready, 1)
                project("u", 3, l)
                pe.wait_ge(rs_ready, l + 1)
                o = free("rb0", l)
                for j in range(4):
                    r = mm(o[:, j * P:(j + 1) * P], rs[:, j:j + 1].to_broadcast([P, P]), ident[:], start=True, stop=True)
                r.then_inc(misc_ready, 1)
                project("b", 4, l)

                pe.wait_ge(dve_emptied, emptied("rb0", l))
                pe.wait_ge(small_full, l * SMALL_LAYER + SMALL_LAYER)

                def cols(v, off, dims):
                    return bass.AP(v.tensor, v.offset + off, [list(v.ap[0])] + dims)

                pe.wait_ge(wuq_ready, l + 1)
                for n, name in enumerate(("qn0", "qn1", "qr", "qrs")):
                    o = free(name, l)
                    for j in range(2):
                        for c in range(2):
                            r = mm(o[:, j * SEQ:(j + 1) * SEQ], wuq[c][:, (2 * n + j) * P:(2 * n + j + 1) * P],
                                   cn[:, c, :], start=c == 0, stop=c == 1)
                    r.then_inc(misc_ready, 1)
                HK = NOPE + MLA_V
                for i in range(2):
                    o = free(f"kn{i}", l)
                    for j in range(4):
                        h = 4 * i + j
                        r = mm(o[64 * (j % 2):64 * (j % 2) + 64, (j // 2) * SEQ:(j // 2 + 1) * SEQ],
                               wukv[:, h * HK:h * HK + NOPE], cn[:, 2, :], start=True, stop=True)
                    r.then_inc(misc_ready, 1)
                for t in range(T):
                    o = free(f"vv{t}", l)
                    mm(o, cn[:, 2, t * P:(t + 1) * P], cols(wukv[:], NOPE, [[HK, 8], [1, MLA_V]]), start=True,
                       stop=True).then_inc(misc_ready, 1)

                pe.wait_ge(act_emptied, emptied("vv1", l))
                pe.wait_ge(rope_ready, l + 1)
                scores(0, l)
                scores(1, l)
                project("c", 5, l)
                scores(2, l)
                scores(3, l)
                pe.wait_ge(ws_masked, l + 1)
                o = free("wst", l)
                for h in range(A_HEADS):
                    r = nc.tensor.transpose(o[:, h * CHUNK:(h + 1) * CHUNK], ws[:, h, :], ident[:])
                r.then_inc(misc_ready, 1)
                project("h", 6, l)
                probs_t(0, l)
                probs_t(1, l)
                scores(4, l)
                scores(5, l)
                project("d", 7, l)
                transpose_x("mt", l, None)
                attend(0, l)
                pe.wait_ge(dve_emptied, emptied("mt3", l))
                project("xk0", K_UNITS[0], l)
                pe.wait_ge(v_ready, l + 1)
                pe.wait_ge(act_emptied, emptied("wst", l))
                o = free("mix", l)
                for h in range(A_HEADS):
                    for t in range(T):
                        c = (h // 2) * SEQ + t * CHUNK
                        r = mm(o[64 * (h % 2):64 * (h % 2) + 64, c:c + CHUNK], vz[:, t, 64 * h:64 * h + 64], wsT[:, h, :],
                               start=True, stop=True)
                r.then_inc(misc_ready, 1)
                probs_t(2, l)
                probs_t(3, l)
                scores(6, l)
                scores(7, l)
                project("xk1", K_UNITS[1], l)
                attend(1, l)
                probs_t(4, l)
                probs_t(5, l)
                project("xk2", K_UNITS[2], l)
                pe.wait_ge(pooled, l + 1)
                o = free("yd", l)
                pe.sem_inc(pe_passed, 1)
                for g in range(4):
                    rows = slice(64 * (g % 2), 64 * (g % 2) + 64)
                    r = mm(o[rows, (g // 2) * SEQ:(g // 2 + 1) * SEQ], pw[rows, g // 2, :], gt[rows, g // 2, :],
                           start=True, stop=True)
                r.then_inc(misc_ready, 1)
                def out_unit(i, need):
                    c0, n = OUT_CHUNKS[i]
                    pe.wait_ge(y_ready, l * 11 + need)
                    into_quad(y_hi, y_lo, c0, n, U_OUT + i, l, i == 0, i == len(OUT_CHUNKS) - 1)

                out_unit(0, 1)
                attend(2, l)
                probs_t(6, l)
                probs_t(7, l)
                out_unit(1, 3)
                attend(3, l)
                out_unit(2, 5)
                out_unit(3, 5)
                out_unit(4, 6)
                out_unit(5, 7)
                project("xk3", K_UNITS[3], l)
                pe.wait_ge(quad_free, l * (3 * T) + T)
                for i in range(4):
                    into_quad(x_hi, x_lo, 2 * i, 2, U_V + i, l, i == 0, i == 3, values=True)
                transpose_x("xb", l, 1)
                pe.wait_ge(dve_emptied, emptied("xb3", l))
                for i in range(4):
                    project(f"xq{i}", U_Q + i, l)
                pe.wait_ge(values_moved, l + 1)
                for h in range(X_HEADS):
                    o = free(f"cs{h}", l)
                    pe.wait_ge(act_emptied, emptied(f"xq{h}", l))
                    for t in range(T):
                        for c in range(2):
                            r = mm(o[:, t * 256:(t + 1) * 256], qT[:, 2 * h + c, t * P:(t + 1) * P], kT[:, 2 * h + c, :],
                                   start=c == 0, stop=c == 1)
                    r.then_inc(misc_ready, 1)
                def x_probs_t(h):
                    pe.wait_ge(xprobs_ready, l * X_HEADS + (h + 1))
                    o = free(f"cpt{h}", l)
                    for m in range(2):
                        for t in range(T):
                            c = 256 * m + 128 * t
                            r = nc.tensor.transpose(o[:, c:c + P], xprobs[:, h, 256 * t + 128 * m:256 * t + 128 * m + P],
                                                    ident[:])
                    r.then_inc(misc_ready, 1)

                x_probs_t(0)
                for h in range(X_HEADS):
                    if h + 1 < X_HEADS:
                        x_probs_t(h + 1)
                    o = free(f"cpv{h}", l)
                    pe.wait_ge(act_emptied, emptied(f"cpt{h}", l))
                    for c in range(2):
                        for m in range(2):
                            r = mm(o[:, c * SEQ:(c + 1) * SEQ], xv[:, m, 256 * h + 128 * c:256 * h + 128 * c + P],
                                   xprobsT[:, h % 2, 256 * m:256 * m + 256], start=m == 0, stop=m == 1)
                    r.then_inc(misc_ready, 1)
                for i in range(4):
                    pe.wait_ge(y_ready, l * 11 + (8 + i))
                    into_quad(y_hi, y_lo, 2 * i, 2, U_O + i, l, i == 0, i == 3)
                transpose_x("xc", l, 2)
                pe.wait_ge(dve_emptied, emptied("xc3", l))
                o = free("rt0", l)
                for k in range(DC):
                    r = three(o[:, 0:SEQ], rw[:, k * E:k * E + P], rw[:, P + k * E:2 * P + k * E], x_hi[:, k, :],
                              x_lo[:, k, :], k == 0, k == DC - 1)
                r.then_inc(misc_ready, 1)
                o = free("rt1", l)
                pe.wait_ge(act_emptied, emptied("rt0", l))
                for t in range(T):
                    r = nc.tensor.transpose(o[:, t * P:(t + 1) * P], logitsT[:, t * P:(t + 1) * P], ident[:])
                r.then_inc(misc_ready, 1)
                pe.wait_ge(member_ready, l + 1)
                counts = bank("rt0")[:, 256:256 + 3 * N_GROUPS]
                every = ones[:, 0:1].to_broadcast([P, P])
                member = [rt[:, 5, 1, 0:8].rearrange("p (t g) -> p t g", t=T)[:, t, :] for t in range(T)]
                mm(counts[:, 0:8], before[:], rt[:, 5, 1, 0:8], start=True, stop=False, skip_group_check=True)
                mm(counts[:, 4:8], every, member[0], start=False, stop=True, skip_group_check=True)
                mm(counts[:, 8:12], every, member[0], start=True, stop=False)
                mm(counts[:, 8:12], every, member[1], start=False, stop=True).then_inc(placed, 1)

                pe.wait_ge(fits_ready, l + 1)
                pe.sem_inc(pe_passed, 1)
                with pe.If(pe.value_load(fits[0:1, 0:1], min_val=0, max_val=1)):
                    pe.sem_inc(misc_ready, 8)

                    def gather(pair):
                        for r in range(4):
                            if r < 2 and pair:
                                pe.wait_ge(dve_emptied, l * DVE_LAYER + (DVE_AHEAD + E - 1 + r))
                            elif pair:
                                pe.wait_ge(gath_lo, l * 8 + (4 * pair + r - 1))
                            for c in range(2):
                                o = gather_bank(pair, r)[:, c * 2 * P:(c + 1) * 2 * P]
                                for t in range(T):
                                    sl = (y_hi, y_lo)[t][:, 8 + pair, :]
                                    mm(o, xn_hi[:, t, 2 * r + c, :], sl, start=t == 0, stop=False)
                                    last = mm(o, xn_lo[:, t, 2 * r + c, :], sl, start=False, stop=t == T - 1)
                            last.then_inc(gathered, 1)

                    def project_slots(b, u, g):
                        pe.wait_ge(split_done, split(u, l))
                        h, lw = unit_views(u, DC, FF)
                        s = slice(P * (g % 2), P * (g % 2) + P)
                        for c in range(DC):
                            r = three(ring[:, b, 0:FF], x_hi[:, c, s], x_lo[:, c, s], h[:, c, :], lw[:, c, :],
                                      c == 0, c == DC - 1)
                        r.then_inc(unit_used, 1)

                    def turn(k):
                        pe.wait_ge(dve_emptied, l * DVE_LAYER + (DVE_AHEAD + 2 * (k + 1)))
                        for c in range(2):
                            r = nc.tensor.transpose(ring[:, 1, FF + c * P:FF + (c + 1) * P],
                                                    s_t[:, k % 2, c * P:(c + 1) * P], ident[:])
                        r.then_inc(turned, 1)

                    def down(k):
                        pe.wait_ge(split_done, split(down_unit(k), l))
                        pe.wait_ge(h_ready, l * E + (k + 1))
                        if k % PER_GROUP == 0 and k:
                            pe.wait_ge(out_split, l * N_GROUPS + k // PER_GROUP)
                        h, lw = unit_views(down_unit(k), 2, D)
                        for a in range(2):
                            for c in range(2):
                                s = slice(c * P, (c + 1) * P)
                                r = three(ring[:, 2 + a, :], y_hi[:, k % 2, s], y_lo[:, k % 2, s],
                                          h[:, c, 512 * a:512 * a + 512], lw[:, c, 512 * a:512 * a + 512],
                                          k % PER_GROUP == 0 and c == 0, k % PER_GROUP == PER_GROUP - 1 and c == 1)
                            if k % PER_GROUP == PER_GROUP - 1 and a == 0:
                                r.then_inc(half_out, 1)
                        r.then_inc(unit_used, 1)

                    def scatter(g):
                        pe.wait_ge(out_split, l * N_GROUPS + (g + 1))
                        for t in range(T):
                            for a in range(2):
                                for i, y in enumerate((y_hi, y_lo)):
                                    r = mm(quad[:, 2 * t + a, :], to_token[:, g, t * P:(t + 1) * P],
                                           y[:, 2 + 2 * a:4 + 2 * a, :].rearrange("p a b -> p (a b)"),
                                           start=g == 0 and i == 0, stop=g == N_GROUPS - 1 and i == 1)
                            if g == N_GROUPS - 1 and t == 0:
                                r.then_inc(quad_ready, 1)
                        return r

                    def to_token_turns():
                        for g in range(N_GROUPS):
                            for t in range(T):
                                c = (g % 2) * SEQ + t * P
                                r = nc.tensor.transpose(ring[:, 2 + g // 2, c:c + P],
                                                        to_slot(t)[:, g * P:(g + 1) * P].bitcast(F32), ident[:])
                        r.then_inc(to_token_done, 1)

                    pe.wait_ge(slots_ready, l * 2 + 1)
                    pe.wait_ge(xn_lo_done, l + 1)
                    gather(0)
                    pe.wait_ge(gates_ready, l + 1)
                    pe.wait_ge(slots_ready, l * 2 + 2)
                    pe.wait_ge(quad_free, l * (3 * T) + 2 * T)
                    for g in range(N_GROUPS):
                        for t in range(T):
                            r = mm(quad[:, 0, 4 * g:4 * g + 4], to_slot(t)[:, g * P:(g + 1) * P].bitcast(F32),
                                   gates[:, t, 4 * g:4 * g + 4], start=t == 0, stop=t == T - 1)
                    r.then_inc(slot_gated, 1)
                    pe.wait_ge(gath_lo, l * 8 + 4)
                    for k in range(E):
                        if k == E // 2:
                            gather(1)
                            pe.wait_ge(gath_lo, l * 8 + 8)
                        elif k:
                            pe.wait_ge(dve_emptied, l * DVE_LAYER + (DVE_AHEAD + 2 * k - 1))
                        project_slots(0, gate_unit(k), k // PER_GROUP)
                        if k:
                            turn(k - 1)
                        else:
                            to_token_turns()
                        if k == 2:
                            pe.wait_ge(to_token_moved, l + 1)
                        if k >= 6 and k % PER_GROUP == 2:
                            scatter(k // PER_GROUP - 1)
                        if k >= 2:
                            down(k - 2)
                        if k:
                            pe.wait_ge(h_ready, l * E + k)
                        project_slots(1, up_unit(k), k // PER_GROUP)
                    down(E - 2)
                    turn(E - 1)
                    down(E - 1)
                    scatter(N_GROUPS - 1).then_inc(moe_done, 1)
                with pe.Else():
                    pe.wait_ge(gates_ready, l + 1)
                    for i in range(8):
                        o = free(f"gb{i}", l)
                        for j in range(2):
                            for t in range(T):
                                r = mm(o[:, j * SEQ + t * P:j * SEQ + (t + 1) * P],
                                       gates[:, t, 2 * i + j:2 * i + j + 1].to_broadcast([P, P]), ident[:],
                                       start=True, stop=True)
                        r.then_inc(misc_ready, 1)

                    def moe_in(b, u, i):
                        pe.wait_ge(split_done, split(u, l) + i)
                        for c in range(2):
                            r = rows_out(ring[:, b, c * SEQ:(c + 1) * SEQ], u, lambda v: v[:, c * P:(c + 1) * P], l)
                        r.then_inc(unit_used, 1)

                    def moe_down(par, u, i, e, first=False, last=False):
                        pe.wait_ge(h_ready, l * E + (e + 1))
                        into_quad(y_hi, y_lo, 2 * par, 2, u, l, first, last, i)

                    pe.wait_ge(act_emptied, emptied("gb7", l))
                    for k in range(2):
                        moe_in(2 * k, gate_unit(k), 0)
                        moe_in(2 * k + 1, up_unit(k), 0)
                    pe.wait_ge(quad_free, l * (3 * T) + 2 * T)

                    def step(k, i, e, first=False):
                        pe.wait_ge(dve_emptied, l * DVE_LAYER + e * 2 + (DVE_AHEAD + 2 * k - 2))
                        moe_in(2 * (k % 2), gate_unit(k), i)
                        moe_down(k % 2, down_unit(k - 2), i, e + (k - 2), first=first)
                        moe_in(2 * (k % 2) + 1, up_unit(k), i)

                    step(2, 0, 0, first=True)
                    step(3, 0, 0)
                    with pe.Fori(1, STEPS) as i:
                        step(2, i * 6, i * 2)
                        step(3, i * 6, i * 2)
                    moe_down(0, down_unit(E - 2), 0, E - 2)
                    moe_down(1, down_unit(E - 1), 0, E - 1, last=True)
                    pe.sem_inc(gathered, 8)
                    pe.sem_inc(slot_gated, 1)
                    pe.sem_inc(to_token_done, 1)
                    pe.sem_inc(turned, E)
                    pe.sem_inc(half_out, N_GROUPS)
                    pe.drain().then_inc(moe_done, 1)


_INS = ['x', 'mem', 'positions', 'w_in', 'gmlp_v_norm_g', 'gmlp_w_s', 'gmlp_b_s', 'mla_q_norm_g', 'mla_w_uq',
        'mla_kv_norm_g', 'mla_w_ukv', 'conv_w', 'pool_w', 'pool_scale', 'w_out', 'ln1_g', 'ln1_b', 'xattn_wq',
        'xattn_wk', 'xattn_wv', 'xattn_wo', 'ln2_g', 'ln2_b', 'router_w', 'router_b', 'moe_w_gate', 'moe_w_up',
        'moe_w_down', 'ln3_g', 'ln3_b']


def shape_constants():
    half = ROPE // 2
    row = np.arange(P)
    freq = (ROPE_BASE ** (-(2.0 * (row % half)) / ROPE)).astype(np.float32)
    sign = np.where(row % ROPE < half, -1.0, 1.0).astype(np.float32)
    inv = np.zeros((P, 2, PAD + 1), np.float32)
    for g, w in enumerate(POOL_WINDOWS):
        rows = slice(64 * (g % 2), 64 * (g % 2) + 64)
        inv[rows, g // 2, 0] = 1.0 / w
        inv[rows, g // 2, 1:] = w / np.minimum(np.arange(1, PAD + 1), w)
    n = np.arange(PER_GROUP)
    order = (n[None, :] < n[:, None]).astype(np.float32)
    order = np.ascontiguousarray(np.broadcast_to(order, (P, *order.shape)))
    return {"rope_freq": freq, "rope_sign": sign, "pool_inv": inv, "pair_order": order}


def kernel(**inputs):
    import concourse.bacc as _bacc
    from concourse.bass_utils import run_bass_kernel_spmd as _run

    nc = _bacc.Bacc("TRN2", target_bir_lowering=False, num_devices=1)
    arrays, args = {}, []
    given = {name: np.ascontiguousarray(inputs[name]) for name in _INS}
    for name, a in {**given, **shape_constants()}.items():
        arrays[f"in_{name}"] = a
        args.append(nc.dram_tensor(f"in_{name}", a.shape, mybir.dt.from_np(a.dtype), kind="ExternalInput").ap())
    shape = inputs["x"].shape
    args.append(nc.dram_tensor("out_x", list(shape), F32, kind="ExternalOutput").ap())
    hybrid_trunk_kernel(nc, *args)
    r = _run(nc, [arrays], core_ids=[0])
    return r.results[0]["out_x"]
```
